# Optimizing a Trainium2 kernel written in Bass

```python
import jax, jax.numpy as jnp
from jax import lax
import numpy as np

D_MODEL = 1024
BATCH = 1
SEQ = 128
DEPTH = 2
DEC_BATCH = 1
DEC_SEQ = 128
PAST_LEN = 128

GRID_W = 64
N_HEADS = 16
HEAD_DIM = D_MODEL // N_HEADS
D_DECAY_LORA = 64
D_AAA_LORA = 64
D_GATE_LORA = 128
GN_EPS = 64e-5
RMS_EPS = 1e-6
WIN_H = 8
WIN_W = 16
Q_COLS = 16
K_SPAN = Q_COLS + WIN_W
D_FF = 2816
N_EXPERTS = 8
TOP_K = 2
D_FF_EXPERT = 2816
ATTN_SCALE = HEAD_DIM ** -0.5

kernel_name = 'hybrid_rwkv7_natten_flow_step'

def rms_norm(x, g):
    xf = x.astype(jnp.float32)
    y = xf * lax.rsqrt(jnp.mean(xf * xf, axis=-1, keepdims=True) + RMS_EPS)
    return (y * g.astype(jnp.float32)).astype(x.dtype)

def adaln(cond, mod_w, mod_b):
    m = jax.nn.silu(cond) @ mod_w + mod_b
    return jnp.split(m[:, None, :], 6, axis=-1)

def modulate(x, g, shift, scale):
    return rms_norm(x, g) * (1 + scale) + shift

def swiglu(x, wg, wu, wd):
    return (jax.nn.silu(x @ wg) * (x @ wu)) @ wd

def top2_moe_swiglu(x, router_w, router_b, exp_wg, exp_wu, exp_wd):
    B, T, D = x.shape
    xt = x.reshape(B * T, D)
    logits = (xt @ router_w).astype(jnp.float32) + router_b.astype(jnp.float32)
    probs = jax.nn.softmax(logits, axis=-1)
    top_p, top_i = lax.top_k(probs, TOP_K)
    top_p = top_p / jnp.sum(top_p, axis=-1, keepdims=True)
    combine = jnp.sum(jax.nn.one_hot(top_i, N_EXPERTS, dtype=jnp.float32) * top_p[..., None], axis=1).astype(x.dtype)
    out = jnp.zeros_like(xt)
    for e in range(N_EXPERTS):
        out = out + combine[:, e:e + 1] * swiglu(xt, exp_wg[e], exp_wu[e], exp_wd[e])
    return out.reshape(B, T, D)

def centred_shift_delta(x):
    prev = jnp.pad(x[:, :-1], ((0, 0), (1, 0), (0, 0)))
    nxt = jnp.pad(x[:, 1:], ((0, 0), (0, 1), (0, 0)))
    return 0.5 * (prev + nxt) - x

def _rwkv7_step(S, inp):
    r, w, k, v, kk, a = inp
    sa = jnp.einsum('bdhij,bdhj->bdhi', S, -kk)
    S = S * w[..., None, :] + sa[..., None] * (kk * a)[..., None, :] + v[..., None] * k[..., None, :]
    return S, jnp.einsum('bdhij,bdhj->bdhi', S, r)

def rwkv7_time_mix(h, S0, mu, wr, wk, wv, wo, w0, w1, w2, a0, a1, a2, g1, g2, k_k, k_a, r_k, lnx_w, lnx_b):
    B, T, D = h.shape
    H, N = N_HEADS, HEAD_DIM
    xx = centred_shift_delta(h)
    xs = h[None] + xx[None] * mu[:, None, None, :]
    xr, xw, xk, xv, xa, xg = xs[0], xs[1], xs[2], xs[3], xs[4], xs[5]
    r = xr @ wr
    k = xk @ wk
    v = xv @ wv
    g = jax.nn.sigmoid(xg @ g1) @ g2
    dw = jnp.einsum('ebtl,eld->ebtd', jnp.tanh(jnp.einsum('btd,edl->ebtl', xw, w1)), w2)
    logw = -jax.nn.softplus(-(w0[:, None, None, :] + dw)) - 0.5
    decay = jnp.exp(-jnp.exp(logw.astype(jnp.float32)))
    a = jax.nn.sigmoid(a0[:, None, None, :] + jnp.einsum('ebtl,eld->ebtd', jnp.einsum('btd,edl->ebtl', xa, a1), a2))
    kd = k[None] * (1 + (a - 1) * k_a)
    kk = (k * k_k).reshape(B, T, H, N).astype(jnp.float32)
    kk = (kk / jnp.maximum(jnp.sqrt(jnp.sum(kk * kk, axis=-1, keepdims=True)), 1e-12)).reshape(B, T, D)

    def dirs(x2):
        x2 = jnp.stack([x2[0], x2[1][:, ::-1]], axis=0)
        return jnp.transpose(x2, (2, 1, 0, 3)).reshape(T, B, 2, H, N).astype(jnp.float32)

    def both(x1):
        return dirs(jnp.stack([x1, x1], axis=0))

    inputs = (both(r), dirs(decay), dirs(kd), both(v), both(kk), dirs(a))
    S_fin, ys = lax.scan(_rwkv7_step, S0.astype(jnp.float32), inputs)
    y = jnp.transpose(ys[:, :, 0] + ys[::-1, :, 1], (1, 0, 2, 3))
    mean = jnp.mean(y, axis=-1, keepdims=True)
    var = jnp.mean(jnp.square(y - mean), axis=-1, keepdims=True)
    y = ((y - mean) * lax.rsqrt(var + GN_EPS)).reshape(B, T, D) * lnx_w + lnx_b
    rh = r.reshape(B, T, H, N).astype(jnp.float32)
    coef = jnp.sum(rh[None] * kd.reshape(2, B, T, H, N).astype(jnp.float32) * r_k, axis=(0, -1))[..., None]
    bonus = (coef * v.reshape(B, T, H, N).astype(jnp.float32)).reshape(B, T, D)
    out = ((y + bonus).astype(h.dtype) * g) @ wo
    return out, S_fin

def split_heads(x):
    B, T, _ = x.shape
    return x.reshape(B, T, N_HEADS, HEAD_DIM).transpose(0, 2, 1, 3)

def merge_heads(x):
    B, H, T, N = x.shape
    return x.transpose(0, 2, 1, 3).reshape(B, T, H * N)

def context_attention(h, wqkv, wo):
    q, k, v = [split_heads(t) for t in jnp.split(h @ wqkv, 3, axis=-1)]
    s = jnp.einsum('bhqn,bhkn->bhqk', q, k).astype(jnp.float32) * ATTN_SCALE
    p = jax.nn.softmax(s, axis=-1).astype(v.dtype)
    o = jnp.einsum('bhqk,bhkn->bhqn', p, v)
    return merge_heads(o) @ wo, k, v

def latent_neighbourhood_attention(h, ctx_k, ctx_v, wqkv, wo, rpb):
    B, T, D = h.shape
    n_rows = T // GRID_W
    kh = min(WIN_H, n_rows)
    ncb = GRID_W // Q_COLS
    q, k, v = [split_heads(t) for t in jnp.split(h @ wqkv, 3, axis=-1)]
    row_ids = jnp.arange(n_rows)
    rows = jnp.clip(row_ids - kh // 2, 0, n_rows - kh)[:, None] + jnp.arange(kh)[None]
    span0 = jnp.clip(jnp.arange(ncb) * Q_COLS - WIN_W // 2, 0, GRID_W - K_SPAN)
    cols = span0[:, None] + jnp.arange(K_SPAN)[None]
    kg = k.reshape(B, N_HEADS, n_rows, GRID_W, HEAD_DIM)
    vg = v.reshape(B, N_HEADS, n_rows, GRID_W, HEAD_DIM)
    ri, ci = rows[:, None, :, None], cols[None, :, None, :]
    kb = kg[:, :, ri, ci]
    vb = vg[:, :, ri, ci]
    qb = q.reshape(B, N_HEADS, n_rows, ncb, Q_COLS, HEAD_DIM)
    qcol = (jnp.arange(ncb) * Q_COLS)[:, None] + jnp.arange(Q_COLS)[None]
    ws = jnp.clip(qcol - WIN_W // 2, 0, GRID_W - WIN_W)[..., None]
    kcol = cols[:, None, :]
    valid = (kcol >= ws) & (kcol < ws + WIN_W)
    ridx = rows - row_ids[:, None] + WIN_H - 1
    cidx = jnp.clip(kcol - qcol[..., None] + WIN_W - 1, 0, 2 * WIN_W - 2)
    bias = rpb[:, ridx[:, None, None, :, None], cidx[None, :, :, None, :]].astype(jnp.float32)
    bias = jnp.where(valid[None, None, :, :, None, :], bias, -jnp.inf)
    s_w = jnp.einsum('bhrcqn,bhrcksn->bhrcqks', qb, kb).astype(jnp.float32) * ATTN_SCALE + bias[None]
    s_c = jnp.einsum('bhrcqn,bhln->bhrcql', qb, ctx_k).astype(jnp.float32) * ATTN_SCALE
    nw = kh * K_SPAN
    s = jnp.concatenate([s_w.reshape(s_w.shape[:5] + (nw,)), s_c], axis=-1)
    p = jax.nn.softmax(s, axis=-1).astype(v.dtype)
    p_w = p[..., :nw].reshape(s_w.shape)
    p_c = p[..., nw:]
    o = jnp.einsum('bhrcqks,bhrcksn->bhrcqn', p_w, vb) + jnp.einsum('bhrcql,bhln->bhrcqn', p_c, ctx_v)
    o = o.reshape(B, N_HEADS, T, HEAD_DIM)
    return merge_heads(o) @ wo

def setup_inputs(seed: int = 0) -> dict:
    key = jax.random.key(seed)
    ks = iter(jax.random.split(key, 64))
    D, H, N = D_MODEL, N_HEADS, HEAD_DIM

    def nrm(shape, scale=1.0):
        return scale * jax.random.normal(next(ks), shape, jnp.float32)

    def gain(shape):
        return 1.0 + nrm(shape, 0.05)

    inp = {}
    inp['x_prompt'] = nrm((BATCH, SEQ, D))
    inp['x_sample'] = nrm((DEC_BATCH, DEC_SEQ, D))
    inp['state_l0'] = nrm((DEC_BATCH, 2, H, N, N), 0.5)
    inp['cache_k_l1'] = nrm((DEC_BATCH, H, PAST_LEN, N))
    inp['cache_v_l1'] = nrm((DEC_BATCH, H, PAST_LEN, N))
    inp['c'] = nrm((DEC_BATCH, D))
    inp['c_ctx'] = nrm((D,))
    inp['l0_mod_w'] = nrm((D, 6 * D), 0.5 * D ** -0.5)
    inp['l0_mod_b'] = nrm((6 * D,), 0.02)
    inp['l0_norm_mix_pre'] = gain((D,))
    inp['l0_norm_mix_post'] = gain((D,))
    inp['l0_norm_ffn_pre'] = gain((D,))
    inp['l0_norm_ffn_post'] = gain((D,))
    inp['l0_mu'] = jax.random.uniform(next(ks), (6, D), jnp.float32)
    inp['l0_wr'] = nrm((D, D), D ** -0.5)
    inp['l0_wk'] = nrm((D, D), D ** -0.5)
    inp['l0_wv'] = nrm((D, D), D ** -0.5)
    inp['l0_wo'] = nrm((D, D), D ** -0.5)
    inp['l0_w0'] = nrm((2, D), 0.5)
    inp['l0_w1'] = nrm((2, D, D_DECAY_LORA), D ** -0.5)
    inp['l0_w2'] = nrm((2, D_DECAY_LORA, D), 0.5 * D_DECAY_LORA ** -0.5)
    inp['l0_a0'] = nrm((2, D), 0.5)
    inp['l0_a1'] = nrm((2, D, D_AAA_LORA), D ** -0.5)
    inp['l0_a2'] = nrm((2, D_AAA_LORA, D), 0.5 * D_AAA_LORA ** -0.5)
    inp['l0_g1'] = nrm((D, D_GATE_LORA), D ** -0.5)
    inp['l0_g2'] = nrm((D_GATE_LORA, D), D_GATE_LORA ** -0.5)
    inp['l0_k_k'] = 0.85 + nrm((D,), 0.05)
    inp['l0_k_a'] = gain((D,))
    inp['l0_r_k'] = nrm((H, N), 0.1)
    inp['l0_lnx_w'] = gain((D,))
    inp['l0_lnx_b'] = nrm((D,), 0.02)
    inp['l0_ffn_wg'] = nrm((D, D_FF), D ** -0.5)
    inp['l0_ffn_wu'] = nrm((D, D_FF), D ** -0.5)
    inp['l0_ffn_wd'] = nrm((D_FF, D), D_FF ** -0.5)
    inp['l1_mod_w'] = nrm((D, 6 * D), 0.5 * D ** -0.5)
    inp['l1_mod_b'] = nrm((6 * D,), 0.02)
    inp['l1_norm_mix_pre'] = gain((D,))
    inp['l1_norm_mix_post'] = gain((D,))
    inp['l1_norm_ffn_pre'] = gain((D,))
    inp['l1_norm_ffn_post'] = gain((D,))
    inp['l1_wqkv'] = nrm((D, 3 * D), D ** -0.5)
    inp['l1_wo'] = nrm((D, D), D ** -0.5)
    inp['l1_rpb'] = nrm((H, 2 * WIN_H - 1, 2 * WIN_W - 1), 0.1)
    inp['l1_router_w'] = nrm((D, N_EXPERTS), D ** -0.5)
    inp['l1_router_b'] = nrm((N_EXPERTS,), 0.01)
    inp['l1_exp_wg'] = nrm((N_EXPERTS, D, D_FF_EXPERT), D ** -0.5)
    inp['l1_exp_wu'] = nrm((N_EXPERTS, D, D_FF_EXPERT), D ** -0.5)
    inp['l1_exp_wd'] = nrm((N_EXPERTS, D_FF_EXPERT, D), D_FF_EXPERT ** -0.5)
    return inp

def reference(x_prompt, x_sample, state_l0, cache_k_l1, cache_v_l1, c, c_ctx,
              l0_mod_w, l0_mod_b, l0_norm_mix_pre, l0_norm_mix_post, l0_norm_ffn_pre, l0_norm_ffn_post,
              l0_mu, l0_wr, l0_wk, l0_wv, l0_wo, l0_w0, l0_w1, l0_w2, l0_a0, l0_a1, l0_a2, l0_g1, l0_g2,
              l0_k_k, l0_k_a, l0_r_k, l0_lnx_w, l0_lnx_b, l0_ffn_wg, l0_ffn_wu, l0_ffn_wd,
              l1_mod_w, l1_mod_b, l1_norm_mix_pre, l1_norm_mix_post, l1_norm_ffn_pre, l1_norm_ffn_post,
              l1_wqkv, l1_wo, l1_rpb, l1_router_w, l1_router_b, l1_exp_wg, l1_exp_wu, l1_exp_wd):
    mods = [(l0_mod_w, l0_mod_b), (l1_mod_w, l1_mod_b)]
    norms = [(l0_norm_mix_pre, l0_norm_mix_post, l0_norm_ffn_pre, l0_norm_ffn_post),
             (l1_norm_mix_pre, l1_norm_mix_post, l1_norm_ffn_pre, l1_norm_ffn_post)]
    rwkv_params = (l0_mu, l0_wr, l0_wk, l0_wv, l0_wo, l0_w0, l0_w1, l0_w2, l0_a0, l0_a1, l0_a2,
                   l0_g1, l0_g2, l0_k_k, l0_k_a, l0_r_k, l0_lnx_w, l0_lnx_b)

    xp, xs = x_prompt, x_sample
    cond_p = c_ctx[None, :]
    for i in range(DEPTH):
        mw, mb = mods[i]
        n_mix_pre, n_mix_post, n_ffn_pre, n_ffn_post = norms[i]
        sh1p, sc1p, gt1p, sh2p, sc2p, gt2p = adaln(cond_p, mw, mb)
        sh1s, sc1s, gt1s, sh2s, sc2s, gt2s = adaln(c, mw, mb)
        hp = modulate(xp, n_mix_pre, sh1p, sc1p)
        hs = modulate(xs, n_mix_pre, sh1s, sc1s)
        if i % 2 == 0:
            zero_state = jnp.zeros((xp.shape[0], 2, N_HEADS, HEAD_DIM, HEAD_DIM), jnp.float32)
            op, new_state_l0 = rwkv7_time_mix(hp, zero_state, *rwkv_params)
            os_, _ = rwkv7_time_mix(hs, state_l0, *rwkv_params)
        else:
            op, new_k_l1, new_v_l1 = context_attention(hp, l1_wqkv, l1_wo)
            os_ = latent_neighbourhood_attention(hs, cache_k_l1, cache_v_l1, l1_wqkv, l1_wo, l1_rpb)
        xp = xp + gt1p * rms_norm(op, n_mix_post)
        xs = xs + gt1s * rms_norm(os_, n_mix_post)
        hp = modulate(xp, n_ffn_pre, sh2p, sc2p)
        hs = modulate(xs, n_ffn_pre, sh2s, sc2s)
        if i % 2 == 0:
            fp = swiglu(hp, l0_ffn_wg, l0_ffn_wu, l0_ffn_wd)
            fs = swiglu(hs, l0_ffn_wg, l0_ffn_wu, l0_ffn_wd)
        else:
            fp = top2_moe_swiglu(hp, l1_router_w, l1_router_b, l1_exp_wg, l1_exp_wu, l1_exp_wd)
            fs = top2_moe_swiglu(hs, l1_router_w, l1_router_b, l1_exp_wg, l1_exp_wu, l1_exp_wd)
        xp = xp + gt2p * rms_norm(fp, n_ffn_post)
        xs = xs + gt2s * rms_norm(fs, n_ffn_post)
    return (xp, xs, new_state_l0, new_k_l1, new_v_l1)


_drawn_inputs = setup_inputs


def setup_inputs(seed=0):
    import zlib

    import numpy as np

    out = dict(_drawn_inputs(seed))
    spreads = {}
    factors = {'l0_lnx_w': 3.632, 'l0_lnx_b': 4.489, 'l1_norm_ffn_post': 4.198, 'l1_router_b': 3.232}
    for name, (base, spread) in spreads.items():
        noise = np.random.default_rng([zlib.crc32(name.encode()), seed]).standard_normal(out[name].shape)
        drawn = base * np.exp(spread * noise) if base else spread * noise
        out[name] = __import__('jax').numpy.asarray(drawn.astype(out[name].dtype))
    for name, factor in factors.items():
        out[name] = (out[name] * factor).astype(out[name].dtype)
    return out
```

```python
from contextlib import ExitStack

import concourse.bass as bass
import numpy as np
from concourse import mybir

F32 = mybir.dt.float32
BF16 = mybir.dt.bfloat16
I32 = mybir.dt.int32
ALU = mybir.AluOpType
ACT = mybir.ActivationFunctionType
AX = mybir.AxisListType.X

P = 128
D = 1024
H = 16
N = D // H
T = 128
G = 2
TT = G * T
C = D // P
FF = 2816
NF = FF // P
NE = 8
GRID_W, WIN_W = 64, 16
RMS_EPS, GN_EPS = 1e-6, 64e-5
SCALE = N ** -0.5
SLOTS = P
NOVER = (TT * 2) // (SLOTS + 1)
NJ = NE + NOVER + 1
DECAY = float(np.exp(-0.5))
CENTRE = 0.5 * T * DECAY

RING = 11
BLK = 3 * D
HALF = BLK + 512
EXTRA = 2912
MIX_SLOTS = 5
MODS = [list(range(8)), [5, 6, 7, 8, 9, 10, 0, 1]]

COLS = {}
_at = 0
for _n, _w in [("pre_mix0", C), ("post_mix0", C), ("pre_ffn0", C), ("post_ffn0", C),
               ("pre_mix1", C), ("post_mix1", C), ("pre_ffn1", C), ("post_ffn1", C),
               ("mu", 6 * C), ("w0", 2 * C), ("a0", 2 * C), ("k_k", C), ("k_a", C), ("r_k", C),
               ("lnx_w", C), ("lnx_b", C), ("mod_b0", 6 * C), ("mod_b1", 6 * C), ("cond", 2 * C),
               ("router_w", NE * C), ("router_b", NE)]:
    COLS[_n] = (_at, _w)
    _at += _w
NCOLS = _at
KCON = {}
_at = 0
for _n, _w in [("ident", P), ("ones", P), ("heads", P), ("head_mean", P),
               ("seen", 2 * 2 * P), ("pair", 2 * P), ("pairT", 2 * P), ("level", 2 * 5 * P),
               ("window", P), ("slot", P), ("expert", NE), ("expert_rank", NE)]:
    KCON[_n] = (_at, _w)
    _at += _w
NCON = _at


def shape_constants():
    s, t = np.arange(P)[:, None], np.arange(P)[None]
    k = {"ident": s == t, "ones": s + t >= 0, "heads": s // N == t // N, "head_mean": (s // N == t // N) / N}
    k["seen"] = np.stack([s < t, s <= t, s > t, s >= t], 1)

    def off(b, lower):
        same = s // (2 * b) == t // (2 * b)
        odd, even = (s // b) % 2 == 1, (t // b) % 2 == 0
        return same & ((odd & even) if lower else (~odd & ~even))

    k["pair"] = np.stack([off(1, True), off(1, False)], 1)
    k["pairT"] = np.stack([off(1, False), off(1, True)], 1)
    k["level"] = np.stack([off(2 ** n, low) for low in (True, False) for n in range(1, 6)], 1)
    qc, kc = s % GRID_W, t % GRID_W
    ws = np.clip(qc - WIN_W // 2, 0, GRID_W - WIN_W)
    k["window"] = np.where((kc >= ws) & (kc < ws + WIN_W), 0.0, -1e30)
    k["slot"] = t + 0 * s
    k["expert"] = np.arange(NE)[None] + 0 * s
    k["expert_rank"] = NE - np.arange(NE)[None] + 0 * s
    return np.concatenate([np.asarray(k[n], np.float32).reshape(P, w) for n, (_, w) in KCON.items()], 1)


class Order:

    def __init__(self, eng, sem):
        self.eng, self.sem, self.before, self.n, self.lead = eng, sem, 0, 0, 0

    def __call__(self, ins):
        ins.then_inc(self.sem, 1)
        self.n += 1
        self.eng.wait_ge(self.sem, self.lead + self.n)

    def enter(self, i, per):
        self.before, self.n, self.per = self.before + self.n, 0, per
        self.lead = self.before + i * per

    def leave(self, turns):
        if self.n != self.per:
            raise ValueError(f"the loop has {self.n} steps, not {self.per}")
        self.before += turns * self.per
        self.n, self.lead = 0, self.before


STEPS_DVE_MIX = 16
STEPS_ACT_MIX = 6
STEPS_POOL_MIX = 22
STEPS_DVE_ATT = 4
STEPS_DVE_JOB = 1


def build(nc, a):
    with ExitStack() as ctx:
        def sb(name, cols, dt=F32):
            return ctx.enter_context(nc.sbuf_tensor(name, [P, cols], dt))[:, :]

        def sem(name):
            return ctx.enter_context(nc.semaphore(name))

        W = sb("W", RING * BLK)
        XT = sb("XT", C * TT).rearrange("p (c t) -> p c t", c=C)
        HT = sb("HT", C * TT).rearrange("p (c t) -> p c t", c=C)
        B = [sb(f"B{i}", C * TT).rearrange("p (c t) -> p c t", c=C) for i in range(3)]
        COL = sb("COL", NCOLS)
        CON = sb("CON", NCON)
        STATE0 = sb("STATE0", C * 2 * N)
        MOD = sb("MOD", 2 * 6 * C * G).rearrange("p (l j g) -> p l j g", l=2, g=G)
        COND = sb("COND", C * G).rearrange("p (c g) -> p c g", g=G)
        GAIN = sb("GAIN", 4 * 2 * C * G).rearrange("p (l k c g) -> p l k c g", l=2, k=4, g=G)
        RMS = sb("RMS", TT)
        RSTD = sb("RSTD", TT)
        BIASES = sb("BIASES", 4)
        ZERO = sb("ZERO", P, BF16)
        HID = sb("HID", 3 * TT).rearrange("p (n t) -> p n t", n=3)
        PAIR = sb("PAIR", C * 10).rearrange("p (c n) -> p c n", n=10)
        PS = [ctx.enter_context(nc.psum_tensor(f"PS{i}", [P, 512], F32))[:, :] for i in range(8)]

        def col(name):
            at, w = COLS[name]
            return COL[:, at:at + w]

        def con(name):
            at, w = KCON[name]
            return CON[:, at:at + w]

        IDENT, ONES, HEADS, HMEAN = con("ident"), con("ones"), con("heads"), con("head_mean")
        SEEN = con("seen").rearrange("p (e k t) -> p e k t", e=2, k=2)
        PAIRM = con("pair").rearrange("p (e t) -> p e t", e=2)
        PAIRT = con("pairT").rearrange("p (e t) -> p e t", e=2)
        LEVEL = con("level").rearrange("p (e n t) -> p e n t", e=2, n=5)

        def slot(s):
            return W[:, s * BLK:(s + 1) * BLK]

        extra = sb("extra", EXTRA)
        areas = {}

        def scratch(phase, cols):
            at = areas.setdefault(phase, [MIX_SLOTS * BLK, 0])
            if at[0] + cols <= RING * BLK:
                at[0] += cols
                return W[:, at[0] - cols:at[0]]
            at[1] += cols
            if at[1] > EXTRA:
                raise ValueError(f"phase {phase} needs {at[1]} floats")
            return extra[:, at[1] - cols:at[1]]

        def two(ap):
            return ap.rearrange("p (e t) -> p e t", e=2)

        AR = [[scratch(0, 2 * TT).rearrange("p (k t) -> p k t", k=2) for _ in range(2)] for _ in range(2)]
        BT = [two(scratch(0, 2 * TT)) for _ in range(2)]
        KT = [two(scratch(0, 2 * TT)) for _ in range(2)]
        GATE = [scratch(0, TT) for _ in range(2)]
        BONUS = [scratch(0, TT) for _ in range(2)]
        VN = [scratch(0, TT).rearrange("p (g i) -> p g i", g=G) for _ in range(2)]
        HATN = [scratch(0, 4 * P).rearrange("p (n j) -> p n j", n=4) for _ in range(2)]
        S0P = [scratch(0, 2 * N).rearrange("p (e i) -> p e i", e=2) for _ in range(2)]
        PP = [scratch(0, 10) for _ in range(2)]
        RKV = scratch(0, 3 * TT).rearrange("p (n t) -> p n t", n=3)
        KKR = scratch(0, TT)
        SQ = scratch(0, TT)
        KKN, ROOT, RROOT, COEF = KKR, SQ, SQ, SQ
        THW = two(scratch(0, 2 * TT))
        THA = two(scratch(0, 2 * TT))
        LD = two(scratch(0, 2 * TT))
        CUM = two(scratch(0, 2 * TT))
        CUX = two(scratch(0, 2 * TT))
        PW = two(scratch(0, 2 * TT))
        PINV, PX = CUM, CUX
        HATT = scratch(0, 4 * P).rearrange("p (n t) -> p n t", n=4)
        GB = [scratch(0, 8 * P).rearrange("p (q k t) -> p q k t", q=4, k=2) for _ in range(2)]
        GK = [scratch(0, 8 * P).rearrange("p (q k t) -> p q k t", q=4, k=2) for _ in range(2)]
        TN = [scratch(0, 4 * P).rearrange("p (q t) -> p q t", q=4) for _ in range(2)]
        TR = [scratch(0, 4 * P).rearrange("p (q t) -> p q t", q=4) for _ in range(2)]
        Z = [scratch(0, 4 * P).rearrange("p (q t) -> p q t", q=4) for _ in range(2)]
        RHS = [scratch(0, 4 * N).rearrange("p (q i) -> p q i", q=4) for _ in range(2)]
        U = [scratch(0, 4 * N).rearrange("p (q i) -> p q i", q=4) for _ in range(2)]
        WU = RHS
        YT = scratch(0, TT)
        YC = scratch(0, TT)
        YQ = scratch(0, TT)
        YR, YS = YT, YQ
        SFIN = scratch(0, 2 * N)
        XX = W[:, MIX_SLOTS * BLK:MIX_SLOTS * BLK + C * TT]
        LORA = slot(RING - 1)
        QK = [scratch(1, 2 * TT).rearrange("p (n t) -> p n t", n=2) for _ in range(2)]
        VA = [scratch(1, TT).rearrange("p (g i) -> p g i", g=G) for _ in range(2)]
        BIAS = [scratch(1, 6 * P).rearrange("p (h k) -> p h k", h=2) for _ in range(2)]
        SC = scratch(1, 6 * P).rearrange("p (h k) -> p h k", h=2)
        EX = scratch(1, 6 * P).rearrange("p (h k) -> p h k", h=2)
        PN = scratch(1, 6 * P).rearrange("p (h k) -> p h k", h=2)
        PT = scratch(1, 6 * P).rearrange("p (h k) -> p h k", h=2)
        MX = scratch(1, 4).rearrange("p (h s) -> p h s", h=2)
        NMX = scratch(1, 4).rearrange("p (h s) -> p h s", h=2)
        SUM = scratch(1, 4).rearrange("p (h s) -> p h s", h=2)
        RSUM = scratch(1, 4).rearrange("p (h s) -> p h s", h=2)
        areas[2] = [RING * BLK, 0]
        SG = [scratch(2, TT) for _ in range(2)]
        HF = [scratch(2, TT) for _ in range(2)]
        SEL = scratch(2, G * SLOTS).rearrange("p (g s) -> p g s", g=G)
        SELW = scratch(2, G * SLOTS).rearrange("p (g s) -> p g s", g=G)
        SELWT = scratch(2, TT)
        names = ["LG", "EXL", "PR", "RA", "OH1", "PR2", "OH2", "CH", "WT", "PM"]
        RT = {n: scratch(2, G * NE).rearrange("p (g e) -> p g e", g=G) for n in names}
        R2 = [scratch(2, G) for _ in range(8)]
        CNT = scratch(2, 4 * NE).rearrange("p (n e) -> p n e", n=4)
        JOBP = scratch(2, G * NJ).rearrange("p (g j) -> p g j", g=G)
        JOBW = scratch(2, G * NJ).rearrange("p (g j) -> p g j", g=G)
        JOBE = scratch(2, NJ)
        JT = scratch(2, G * NE).rearrange("p (g e) -> p g e", g=G)
        JOBI = sb("JOBI", NJ + 1, I32)
        HN = B[0].rearrange("p c t -> p (c t)").rearrange("p (g d) -> p g d", g=G)
        XS = B[1].rearrange("p c t -> p (c t)")[:, 0:C * SLOTS].rearrange("p (c s) -> p c s", c=C)
        YSB = B[1].rearrange("p c t -> p (c t)")[:, D:2 * D]
        ACC = B[2]

        col_in, con_in, x_in, s0_in = sem("col_in"), sem("con_in"), sem("x_in"), sem("s0_in")
        slot_full = [sem(f"slot_full{i}") for i in range(RING)]
        pair_full = [sem(f"pair_full{i}") for i in range(2)]
        apair_full = [sem(f"apair_full{i}") for i in range(2)]
        wo_full = [sem(f"wo_full{i}") for i in range(2)]
        lora_full = sem("lora_full")
        mod_used = [sem(f"mod_used{i}") for i in range(2)]
        wo_psum = [sem(f"wo_psum{i}") for i in range(2)]
        wo_sbuf = [sem(f"wo_sbuf{i}") for i in range(2)]
        ffn_used, exp_used = sem("ffn_used"), sem("exp_used")
        eps_ready, zero_ready = sem("eps_ready"), sem("zero_ready")
        cond_ready, mod_ready = sem("cond_ready"), sem("mod_ready")
        sq_ready, sum_ready, root_ready = sem("sq_ready"), sem("sum_ready"), sem("root_ready")
        h_ready, x_ready = sem("h_ready"), sem("x_ready")
        mixed_ready, hid_psum, hid_sbuf = sem("mixed_ready"), sem("hid_psum"), sem("hid_sbuf")
        prep_psum, prep_act, prep_pool, prep_dve = (sem("prep_psum"), sem("prep_act"), sem("prep_pool"),
                                                    sem("prep_dve"))
        chain_psum = [sem(f"chain_psum{i}") for i in range(2)]
        chain_sbuf = [sem(f"chain_sbuf{i}") for i in range(2)]
        gn_psum, gn_sbuf, gn_root, z_ready = sem("gn_psum"), sem("gn_sbuf"), sem("gn_root"), sem("z_ready")
        state_ready, state_out = sem("state_ready"), sem("state_out")
        gu_psum, sg_ready, hf_ready, yt_psum = sem("gu_psum"), sem("sg_ready"), sem("hf_ready"), sem("yt_psum")
        yt_sbuf = sem("yt_sbuf")
        qkv_psum, qkv_sbuf, bias_ready = sem("qkv_psum"), sem("qkv_sbuf"), sem("bias_ready")
        kv_out = [sem(f"kv_out{i}") for i in range(2)]
        score_psum, score_ready, exp_ready, prob_ready = (sem("score_psum"), sem("score_ready"),
                                                          sem("exp_ready"), sem("prob_ready"))
        probT_psum, probT_sbuf, att_psum, att_sbuf = (sem("probT_psum"), sem("probT_sbuf"), sem("att_psum"),
                                                      sem("att_sbuf"))
        hn_psum, hn_sbuf, logit_psum, logit_ready, logit_exp = (
            sem("hn_psum"), sem("hn_sbuf"), sem("logit_psum"), sem("logit_ready"), sem("logit_exp"))
        chosen, place_psum, jobs_ready = sem("chosen"), sem("place_psum"), sem("jobs_ready")
        sel_ready, gather_psum, gather_sbuf = sem("sel_ready"), sem("gather_psum"), sem("gather_sbuf")
        selT_psum, selT_sbuf = sem("selT_psum"), sem("selT_sbuf")
        egu_psum, esg_ready, ehf_ready = sem("egu_psum"), sem("esg_ready"), sem("ehf_ready")
        ey_psum, ey_sbuf, scat_psum, scat_acc = sem("ey_psum"), sem("ey_sbuf"), sem("scat_psum"), sem("scat_acc")
        y_out, moe_done = sem("y_out"), sem("moe_done")
        dve_order, last_order, act_order, pool_order = sem("dve_order"), sem("last_order"), sem("act_order"), sem("pool_order")

        CH = 17

        def chunk_slots(r, k):
            return slot((MIX_SLOTS + k) % RING)

        before_ffn = [2 if s < 8 else 0 for s in range(RING)]
        before_mod1 = [n + 2 for n in before_ffn]
        before_exp = [n + 2 * (s in MODS[1]) for s, n in enumerate(before_mod1)]

        block = ctx.enter_context(nc.Block())

        @block.sync
        def _(sp):
            def mod_block(l, n):
                s = MODS[l][n % 8]
                sp.dma_start(slot(s), a["w_mod"][l, n]).then_inc(slot_full[s], 16)

            def pair_block(l, c, p):
                if l == 0:
                    sp.dma_start(W[:, HALF * p:HALF * p + BLK + 384], a["w_rkv"][c]).then_inc(pair_full[p], 16)
                else:
                    sp.dma_start(W[:, HALF * p:HALF * (p + 1)], a["w_qkv"][c]).then_inc(apair_full[p], 16)

            for n in range(16):
                if n >= 8:
                    sp.wait_ge(mod_used[0], n - 7)
                mod_block(0, n)
                if n == 11:
                    sp.dma_start(LORA, a["w_lora"]).then_inc(lora_full, 16)
            sp.wait_ge(mod_used[0], 16)
            pair_block(0, 0, 0)
            pair_block(0, 1, 1)
            sp.dma_start(W[:, 2 * HALF:MIX_SLOTS * BLK], a["w_o"][0]).then_inc(wo_full[0], 16)
            with sp.Fori(0, 3) as i:
                for p in range(2):
                    sp.wait_ge(prep_psum, 6 * (2 * i + p) + 3)
                    sp.dma_start(W[:, HALF * p:HALF * p + BLK + 384],
                                 a["w_rkv"][bass.ds(2 * i + p + 2, 1)].rearrange("a p n -> (a p) n"))\
                      .then_inc(pair_full[p], 16)
            sp.wait_ge(state_ready, C)
            sp.wait_ge(state_out, 16 * C)
            sp.wait_ge(z_ready, C)
            for k in range(RING):
                s = (MIX_SLOTS + k) % RING
                if s == 2:
                    sp.wait_ge(wo_psum[0], 4)
                sp.dma_start(slot(s), a["w_ffn"][k]).then_inc(slot_full[s], 16)
            for k in range(RING):
                s = (MIX_SLOTS + k) % RING
                sp.wait_ge(ffn_used, k + 1)
                sp.dma_start(slot(s), a["w_ffn"][RING + k]).then_inc(slot_full[s], 16)
            for n in range(16):
                if n < 8:
                    sp.wait_ge(ffn_used, RING + 1 + (MODS[1][n] - MIX_SLOTS) % RING)
                else:
                    sp.wait_ge(mod_used[1], n - 7)
                mod_block(1, n)
            sp.wait_ge(ffn_used, NF)
            sp.wait_ge(mod_used[1], 16)
            pair_block(1, 0, 0)
            pair_block(1, 1, 1)
            sp.dma_start(W[:, 2 * HALF:MIX_SLOTS * BLK], a["w_o"][1]).then_inc(wo_full[1], 16)
            with sp.Fori(0, 3) as i:
                for p in range(2):
                    sp.wait_ge(att_psum, 2 * i + p + 1)
                    sp.dma_start(W[:, HALF * p:HALF * (p + 1)],
                                 a["w_qkv"][bass.ds(2 * i + p + 2, 1)].rearrange("a p n -> (a p) n"))\
                      .then_inc(apair_full[p], 16)
            sp.wait_ge(att_sbuf, C)
            sp.wait_ge(kv_out[0], 32 * C // 2)
            sp.wait_ge(kv_out[1], 32 * C // 2)
            for k in range(RING):
                s = (MIX_SLOTS + k) % RING
                if s == 2:
                    sp.wait_ge(wo_psum[1], 4)
                sp.dma_start(slot(s), a["w_exp"][0, k]).then_inc(slot_full[s], 16)

            def exp_blocks(j, e, rounds):
                for r in rounds:
                    for k in range(RING):
                        s = (MIX_SLOTS + k) % RING
                        sp.wait_ge(exp_used, NF * j + RING * (r - 1) + k + 1)
                        src = a["w_exp"][e, RING * r + k] if isinstance(e, int) else \
                            a["w_exp"][bass.ds(e, 1), RING * r + k].rearrange("a p n -> (a p) n")
                        sp.dma_start(slot(s), src).then_inc(slot_full[s], 16)

            exp_blocks(0, 0, [1])
            with sp.Fori(1, NE) as j:
                exp_blocks(j, j, [0, 1])
            sp.wait_ge(jobs_ready, 1)
            over = sp.value_load(JOBI[0:1, NJ:NJ + 1], min_val=0, max_val=NOVER)
            with sp.Fori(0, over) as j:
                e = sp.value_load(JOBI[0:1, bass.ds(j + NE, 1)], min_val=0, max_val=NE - 1)
                exp_blocks(j + NE, e, [0, 1])
            sp.wait_ge(x_ready, 4)
            sp.dma_start(a["out_x"], XT).then_inc(y_out, 16)
            sp.wait_ge(y_out, 16)

        @block.tensor
        def _(pe):
            mm = nc.tensor.matmul

            def modulation(l):
                if l == 0:
                    pe.wait_ge(col_in, 16)
                    pe.wait_ge(cond_ready, 1)
                base = 0 if l == 0 else None
                for r in range(2):
                    for k in range(8):
                        s = MODS[l][k]
                        pe.wait_ge(slot_full[s], 16 * ((before_mod1[s] if l else 0) + r + 1))
                        w = slot(s).rearrange("p (j k m) -> p j k m", j=3, k=C)
                        for jj in range(3):
                            j = 24 * r + 3 * k + jj
                            for kc in range(C):
                                last = mm(PS[0][:, 2 * j:2 * j + 2], w[:, jj, kc], COND[:, kc],
                                          start=(kc == 0), stop=(kc == C - 1))
                        last.then_inc(mod_used[l], 1)

            def norm_sum(n):
                pe.wait_ge(sq_ready, n)
                for c in range(C):
                    last = mm(PS[1][:, 0:TT], ONES, B[1][:, c], start=(c == 0), stop=(c == C - 1))
                last.then_inc(sum_ready, 1)

            def project_out(l, src):
                pe.wait_ge(wo_full[l], 16)
                wo = W[:, 2 * HALF:MIX_SLOTS * BLK].rearrange("p (j k m) -> p j k m", j=C, k=C)
                for b in range(4):
                    if b >= 2:
                        pe.wait_ge(wo_sbuf[l], b - 1)
                    for half in range(2):
                        for kc in range(C):
                            last = mm(PS[2 + b % 2][:, TT * half:TT * half + TT], wo[:, 2 * b + half, kc],
                                      src[:, kc], start=(kc == 0), stop=(kc == C - 1))
                    last.then_inc(wo_psum[l], 1)

            def wblock(p):
                blk = W[:, HALF * p:HALF * (p + 1)]
                return (blk[:, 0:BLK].rearrange("p (n k m) -> p n k m", n=3, k=C),
                        blk[:, BLK:BLK + 384].rearrange("p (n m) -> p n m", n=3))

            def chain(e, c, k, ins):
                ins.then_inc(chain_psum[e], 1)

            def prep_rkv(c, r, p):
                w, w2 = wblock(p)
                pe.wait_ge(pair_full[p], 16 * (r + 1))
                if not (isinstance(c, int) and c == 0):
                    pe.wait_ge(prep_act, 4 * (c - 1) + 2)
                for n in range(2):
                    for kc in range(C):
                        last = mm(PS[4][:, TT * n:TT * n + TT], w[:, n, kc], B[n][:, kc],
                                  start=(kc == 0), stop=(kc == C - 1))
                last.then_inc(prep_psum, 1)
                for kc in range(C):
                    mm(PS[5][:, 0:TT], w[:, 2, kc], B[2][:, kc], start=(kc == 0), stop=(kc == C - 1))
                mm(PS[5][:, TT:2 * TT], w2[:, 2], HID[:, 2], start=True, stop=True).then_inc(prep_psum, 1)

            def prep_lora(c, p):
                _, w2 = wblock(p)
                pe.wait_ge(prep_act, 4 * c + 1)
                for n in range(2):
                    for e in range(2):
                        rows = slice(N * e, N * e + N)
                        last = mm(PS[4 + e][:, TT * n:TT * n + TT], w2[rows, n], HID[rows, n],
                                  start=True, stop=True)
                last.then_inc(prep_psum, 1)

            def prep_norm(c):
                pe.wait_ge(prep_pool, 3 * c + 1)
                if not (isinstance(c, int) and c == 0):
                    pe.wait_ge(prep_dve, 6 * (c - 1) + 6)
                mm(PS[6][:, 0:TT], HEADS, SQ, start=True, stop=True).then_inc(prep_psum, 1)

            def prep_coef(c):
                pe.wait_ge(prep_pool, 3 * c + 3)
                pe.wait_ge(prep_dve, 6 * c + 2)
                mm(PS[6][:, 0:TT], HEADS, COEF, start=True, stop=True)
                for g in range(G):
                    last = nc.tensor.transpose(PS[6][:, TT + P * g:TT + P * g + P], RKV[:, 2, P * g:P * g + P],
                                               IDENT)
                last.then_inc(prep_psum, 1)

            def prep_hat(c):
                pe.wait_ge(prep_dve, 6 * c + 5)
                for n in range(4):
                    last = nc.tensor.transpose(PS[6][:, P * n:P * n + P], HATT[:, n], IDENT)
                last.then_inc(prep_psum, 1)

            def heads(q):
                hl, g = q // 2, q % 2
                return slice(N * hl, N * hl + N), slice(T * g, T * g + T)

            def gram(e, c, p, k):
                if k > 1 or not (isinstance(c, int) and c == 0):
                    pe.wait_ge(chain_sbuf[e], CH * c + k - 1)
                if k == 1:
                    pe.wait_ge(prep_pool, 3 * c + 3)
                for q in range(4):
                    rows, cs = heads(q)
                    bank = PS[2 * e + q // 2]
                    if k < 3:
                        lhs = (BT if k == 1 else KT)[p][rows, e, cs]
                        rhs = AR[p][e][rows, :, cs]
                        out = bank[:, 256 * (q % 2):256 * (q % 2) + 256].rearrange("p (k t) -> p k t", k=2)
                    else:
                        lhs, rhs = AR[p][e][rows, 0, cs], BT[p][rows, e, cs]
                        out = bank[:, P * (q % 2):P * (q % 2) + P]
                    last = mm(out, lhs, rhs, start=True, stop=True)
                last.then_inc(chain_psum[e], 1)

            def level_z(e, c, n):
                pe.wait_ge(chain_sbuf[e], CH * c + 2 * n + 1)
                for q in range(4):
                    last = mm(PS[2 * e][:, P * q:P * q + P], GB[e][:, q, 0], TN[e][:, q], start=True, stop=True)
                last.then_inc(chain_psum[e], 1)

            def level_d(e, c, n):
                pe.wait_ge(chain_sbuf[e], CH * c + 2 * n + 2)
                if n < 5:
                    for q in range(4):
                        mm(PS[2 * e + 1][:, P * q:P * q + P], TR[e][:, q], Z[e][:, q], start=True, stop=True)
                for q in range(4):
                    last = mm(PS[2 * e][:, P * q:P * q + P], Z[e][:, q], TR[e][:, q], start=True, stop=True)
                last.then_inc(chain_psum[e], 1)

            def right_side(e, c, p):
                pe.wait_ge(chain_sbuf[e], CH * c + 13)
                pe.wait_ge(prep_dve, 6 * c + 5)
                for q in range(4):
                    rows, cs = heads(q)
                    out = PS[2 * e + q // 2][:, N * (q % 2):N * (q % 2) + N]
                    mm_last = mm(out, GK[e][:, q, 0], VN[p][:, q % 2, rows], start=True, stop=(q % 2 == 0))
                    if q % 2:
                        mm_last = mm(out, AR[p][e][rows, 0, cs], S0P[p][rows, e], start=False, stop=True)
                mm_last.then_inc(chain_psum[e], 1)

            def solve0(e, c):
                pe.wait_ge(chain_sbuf[e], CH * c + 14)
                for q in range(4):
                    last = mm(PS[2 * e][:, N * q:N * q + N], TR[e][:, q], RHS[e][:, q], start=True, stop=True)
                last.then_inc(chain_psum[e], 1)

            def halves(e):
                return (slice(0, 64), slice(64, 128)) if e == 0 else (slice(64, 128), slice(0, 64))

            def solve1(e, c):
                first, _ = halves(e)
                pe.wait_ge(chain_sbuf[e], CH * c + 15)
                for q in range(4):
                    last = mm(PS[2 * e + 1][:, N * q:N * q + N], GB[e][first, q, 0], U[e][first, q],
                              start=True, stop=True)
                last.then_inc(chain_psum[e], 1)

            def solve2(e, c):
                _, then = halves(e)
                pe.wait_ge(chain_sbuf[e], CH * c + 16)
                for q in range(4):
                    last = mm(PS[2 * e][:, N * q:N * q + N], TR[e][then, q], WU[e][then, q],
                              start=True, stop=True)
                last.then_inc(chain_psum[e], 1)

            def outputs(c, p):
                for e in range(2):
                    pe.wait_ge(chain_sbuf[e], CH * c + 17)
                pe.wait_ge(prep_dve, 6 * c + 6)
                if not (isinstance(c, int) and c == 0):
                    pe.wait_ge(gn_root, c)
                for q in range(4):
                    rows, cs = heads(q)
                    out = PS[7][rows, cs]
                    mm(out, VN[p][:, q % 2, rows], GK[0][:, q, 1], start=True, stop=False)
                    mm(out, VN[p][:, q % 2, rows], GK[1][:, q, 1], start=False, stop=False)
                    if q % 2:
                        mm(out, S0P[p][rows, 0], AR[p][0][rows, 1, cs], start=False, stop=False)
                        mm(out, S0P[p][rows, 1], AR[p][1][rows, 1, cs], start=False, stop=False)
                    mm(out, U[0][:, q], GB[0][:, q, 1], start=False, stop=False)
                    mm(out, U[1][:, q], GB[1][:, q, 1], start=False, stop=True)
                for hl in range(2):
                    for e in range(2):
                        rows = slice(N * hl, N * hl + N)
                        out = PS[7][rows, TT + N * e:TT + N * e + N]
                        mm(out, U[e][:, 2 * hl], HATN[p][:, 2 * e, rows], start=True, stop=False)
                        last = mm(out, VN[p][:, 0, rows], HATN[p][:, 2 * e + 1, rows], start=False, stop=True)
                last.then_inc(gn_psum, 1)

            def gn_mean(c):
                pe.wait_ge(gn_sbuf, 2 * c + 1)
                mm(PS[7][:, 0:TT], HMEAN, YT, start=True, stop=True).then_inc(gn_psum, 1)

            def gn_var(c):
                pe.wait_ge(gn_sbuf, 2 * c + 2)
                mm(PS[7][:, 0:TT], HMEAN, YQ, start=True, stop=True).then_inc(gn_psum, 1)

            def prep_all(c, r, p):
                prep_rkv(c, r, p)
                prep_lora(c, p)
                prep_norm(c)

            def mix_step(c, p, prep, tail):
                r1 = None
                for e in range(2):
                    gram(e, c, p, 1)
                if tail:
                    gn_mean(c - 1)
                if prep is not None:
                    prep_rkv(*prep)
                if tail:
                    gn_var(c - 1)
                for e in range(2):
                    gram(e, c, p, 2)
                if prep is not None:
                    prep_lora(prep[0], prep[2])
                for e in range(2):
                    gram(e, c, p, 3)
                if prep is not None:
                    prep_norm(prep[0])
                for n in range(1, 6):
                    for e in range(2):
                        level_z(e, c, n)
                    for e in range(2):
                        level_d(e, c, n)
                    if prep is not None and n == 4:
                        prep_coef(prep[0])
                if prep is not None:
                    prep_hat(prep[0])
                for e in range(2):
                    right_side(e, c, p)
                for f in (solve0, solve1, solve2):
                    for e in range(2):
                        f(e, c)
                outputs(c, p)

            modulation(0)
            pe.wait_ge(con_in, 16)
            norm_sum(1)
            pe.wait_ge(lora_full, 16)
            w1 = LORA.rearrange("p (n k m) -> p n k m", n=3, k=C)
            for n in range(3):
                pe.wait_ge(mixed_ready, n + 1)
                for kc in range(C):
                    last = mm(PS[2 + n][:, 0:TT], w1[:, n, kc], B[n][:, kc], start=(kc == 0), stop=(kc == C - 1))
                last.then_inc(hid_psum, 1)
            pe.wait_ge(hid_sbuf, 3)
            pe.wait_ge(mixed_ready, 6)
            prep_rkv(0, 0, 0)
            prep_lora(0, 0)
            prep_norm(0)
            prep_coef(0)
            prep_hat(0)
            mix_step(0, 0, (1, 0, 1), False)
            with pe.Fori(0, 3) as i:
                mix_step(2 * i + 1, 1, (2 * i + 2, i + 1, 0), True)
                mix_step(2 * i + 2, 0, (2 * i + 3, i + 1, 1), True)
            mix_step(7, 1, None, True)
            gn_mean(7)
            gn_var(7)
            pe.wait_ge(z_ready, C)
            project_out(0, HT)
            norm_sum(2)
            norm_sum(3)

            def open_banks(banks, start):
                for b in banks:
                    last = mm(PS[b], ZERO, ZERO[:, 0:1].to_broadcast([P, 512]), start=start, stop=not start)
                return last

            pe.wait_ge(h_ready, 2)
            pe.wait_ge(zero_ready, 1)
            open_banks(range(2, 6), True)

            def gate_up(w, k, src, width, done):
                for u in range(2):
                    for kc in range(C):
                        last = mm(PS[k % 2][:, width * u:width * u + width], w[:, u, kc], src[:, kc],
                                  start=(kc == 0), stop=(kc == C - 1))
                last.then_inc(done, 1)

            def ffn_down(k, r):
                pe.wait_ge(hf_ready, RING * r + k + 1)
                wd = slot((MIX_SLOTS + k) % RING)[:, 2 * D:3 * D].rearrange("p (c m) -> p c m", c=C)
                for c in range(C):
                    last = mm(PS[2 + c // 2][:, TT * (c % 2):TT * (c % 2) + TT], wd[:, c], HF[k % 2],
                              start=False, stop=False)
                last.then_inc(ffn_used, 1)

            with pe.Fori(0, 2) as r:
                for k in range(RING):
                    s = (MIX_SLOTS + k) % RING
                    pe.wait_ge(slot_full[s], 16 * (r + before_ffn[s] + 1))
                    w = slot(s)[:, 0:2 * D].rearrange("p (u k m) -> p u k m", u=2, k=C)
                    gate_up(w, k, HT, TT, gu_psum)
                    if k:
                        ffn_down(k - 1, r)
                ffn_down(RING - 1, r)
            open_banks(range(2, 6), False).then_inc(yt_psum, 1)
            modulation(1)
            norm_sum(4)
            norm_sum(5)

            def qkv(c, r, p):
                w = W[:, HALF * p:HALF * p + BLK].rearrange("p (n k m) -> p n k m", n=3, k=C)
                pe.wait_ge(apair_full[p], 16 * (r + 1))
                if not (isinstance(c, int) and c == 0):
                    pe.wait_ge(qkv_sbuf, 2 * c)
                for n in range(2):
                    for kc in range(C):
                        last = mm(PS[0][:, TT * n:TT * n + TT], w[:, n, kc], HT[:, kc],
                                  start=(kc == 0), stop=(kc == C - 1))
                last.then_inc(qkv_psum, 1)
                for g in range(G):
                    for kc in range(C):
                        last = mm(PS[1][:, P * g:P * g + P], HT[:, kc, T * g:T * g + T], w[:, 2, kc],
                                  start=(kc == 0), stop=(kc == C - 1))
                last.then_inc(qkv_psum, 1)

            def attend(c, p, nxt):
                pair = W[:, HALF * p + BLK:HALF * (p + 1)]
                ctx_k, ctx_v = pair[:, 2 * P:3 * P], pair[:, 3 * P:4 * P]
                pe.wait_ge(qkv_sbuf, 2 * c + 2)
                if not (isinstance(c, int) and c == 0):
                    pe.wait_ge(score_ready, c)
                for hl in range(2):
                    rows = slice(N * hl, N * hl + N)
                    for g in range(G):
                        mm(PS[2 + hl][:, P * g:P * g + P], QK[p][rows, 0, T * g:T * g + T],
                           QK[p][rows, 1, T * g:T * g + T], start=True, stop=True)
                    last = mm(PS[2 + hl][:, 2 * P:3 * P], QK[p][rows, 0, T:2 * T], ctx_k[rows],
                              start=True, stop=True)
                last.then_inc(score_psum, 1)
                if nxt is not None:
                    qkv(*nxt)
                pe.wait_ge(prob_ready, c + 1)
                if not (isinstance(c, int) and c == 0):
                    pe.wait_ge(probT_sbuf, c)
                for hl in range(2):
                    for n in range(3):
                        last = nc.tensor.transpose(PS[4 + hl][:, P * n:P * n + P], PN[:, hl, P * n:P * n + P], IDENT)
                last.then_inc(probT_psum, 1)
                pe.wait_ge(probT_sbuf, c + 1)
                if not (isinstance(c, int) and c == 0):
                    pe.wait_ge(att_sbuf, c)
                for hl in range(2):
                    rows = slice(N * hl, N * hl + N)
                    mm(PS[6][rows, 0:T], VA[p][:, 0, rows], PT[:, hl, 0:P], start=True, stop=True)
                    mm(PS[6][rows, T:2 * T], VA[p][:, 1, rows], PT[:, hl, P:2 * P], start=True, stop=False)
                    last = mm(PS[6][rows, T:2 * T], ctx_v[:, rows], PT[:, hl, 2 * P:3 * P], start=False, stop=True)
                last.then_inc(att_psum, 1)

            pe.wait_ge(h_ready, 3)
            qkv(0, 0, 0)
            attend(0, 0, (1, 0, 1))
            with pe.Fori(0, 3) as i:
                attend(2 * i + 1, 1, (2 * i + 2, i + 1, 0))
                attend(2 * i + 2, 0, (2 * i + 3, i + 1, 1))
            attend(7, 1, None)
            pe.wait_ge(att_sbuf, C)
            project_out(1, B[1])
            norm_sum(6)
            norm_sum(7)

            pe.wait_ge(h_ready, 4)
            for g in range(G):
                for c in range(C):
                    last = nc.tensor.transpose(PS[2 * g + c // 4][:, P * (c % 4):P * (c % 4) + P],
                                               HT[:, c, T * g:T * g + T], IDENT)
            last.then_inc(hn_psum, 1)
            rw = col("router_w").rearrange("p (c e) -> p c e", c=C)
            for g in range(G):
                for c in range(C):
                    last = mm(PS[4][:, NE * g:NE * g + NE], HT[:, c, T * g:T * g + T], rw[:, c],
                              start=(c == 0), stop=(c == C - 1))
            last.then_inc(logit_psum, 1)
            pe.wait_ge(chosen, 1)
            ch = RT["CH"]
            mm(PS[5][:, 0:NE], SEEN[:, 0, 0], ch[:, 0], start=True, stop=True)
            mm(PS[5][:, NE:2 * NE], ONES, ch[:, 0], start=True, stop=False)
            mm(PS[5][:, NE:2 * NE], SEEN[:, 0, 0], ch[:, 1], start=False, stop=True)
            mm(PS[5][:, 2 * NE:3 * NE], ONES, ch[:, 0], start=True, stop=False)
            mm(PS[5][:, 2 * NE:3 * NE], ONES, ch[:, 1], start=False, stop=True).then_inc(place_psum, 1)
            pe.wait_ge(hn_sbuf, 1)

            def gather(j):
                pe.wait_ge(sel_ready, j + 1)
                for c in range(C):
                    for g in range(G):
                        last = mm(PS[4 + c // 4][:, P * (c % 4):P * (c % 4) + P], HN[:, g, P * c:P * c + P],
                                  SEL[:, g], start=(g == 0), stop=(g == G - 1))
                last.then_inc(gather_psum, 1)

            def turn_weights(j):
                pe.wait_ge(sel_ready, j + 1)
                for g in range(G):
                    last = nc.tensor.transpose(PS[0][:, P * g:P * g + P], SELW[:, g], IDENT)
                last.then_inc(selT_psum, 1)

            def exp_down(j, r, k):
                pe.wait_ge(ehf_ready, NF * j + RING * r + k + 1)
                wd = slot((MIX_SLOTS + k) % RING)[:, 2 * D:3 * D]
                for half in range(2):
                    last = mm(PS[2 + half], HF[k % 2][:, 0:SLOTS], wd[:, 512 * half:512 * half + 512],
                              start=False, stop=False)
                last.then_inc(exp_used, 1)

            def job(j):
                pe.wait_ge(gather_sbuf, j + 1)
                pe.wait_ge(ey_sbuf, j)
                pe.wait_ge(selT_sbuf, j + 1)
                open_banks((2, 3), True)
                with pe.Fori(0, 2) as r:
                    for k in range(RING):
                        s = (MIX_SLOTS + k) % RING
                        pe.wait_ge(slot_full[s], 16 * (2 * j + r + before_exp[s] + 1))
                        w = slot(s)[:, 0:2 * D].rearrange("p (u k m) -> p u k m", u=2, k=C)
                        gate_up(w, k, XS, SLOTS, egu_psum)
                        if k:
                            exp_down(j, r, k - 1)
                    exp_down(j, r, RING - 1)
                open_banks((2, 3), False).then_inc(ey_psum, 1)
                pe.wait_ge(scat_acc, 4 * j)
                gather(j + 1)
                pe.wait_ge(ey_sbuf, j + 1)
                for b in range(4):
                    bank = PS[(6, 7, 4, 5)[b]]
                    if b == 2:
                        pe.wait_ge(gather_sbuf, j + 2)
                    for half in range(2):
                        c = 2 * b + half
                        last = mm(bank[:, TT * half:TT * half + TT], YSB[:, P * c:P * c + P], SELWT,
                                  start=True, stop=True)
                    last.then_inc(scat_psum, 1)
                turn_weights(j + 1)

            gather(0)
            turn_weights(0)
            with pe.Fori(0, NE) as j:
                job(j)
            over = pe.value_load(JOBI[0:1, NJ:NJ + 1], min_val=0, max_val=NOVER)
            with pe.Fori(0, over) as j:
                job(j + NE)
            norm_sum(8)

        @block.scalar
        def _(act):
            order = Order(act, act_order)
            fn = nc.scalar.activation
            act.dma_start(COL, a["cols"]).then_inc(col_in, 16)
            act.dma_start(XT, a["x"]).then_inc(x_in, 16)
            act.dma_start(CON, a["cons"]).then_inc(con_in, 16)
            act.dma_start(STATE0, a["state0"]).then_inc(s0_in, 16)
            act.wait_ge(col_in, 16)
            fn(COND, col("cond").rearrange("p (c g) -> p c g", g=G), ACT.Silu).then_inc(cond_ready, 1)

            def norm(n, src, free=None):
                fn(B[1], src, ACT.Square).then_inc(sq_ready, 1)
                act.wait_ge(sum_ready, n)
                if n >= 2:
                    act.wait_ge(x_ready if n % 2 else h_ready, n // 2)
                fn(RMS, PS[1][:, 0:TT], ACT.Sqrt, scale=1.0 / D, bias=BIASES[:, 0:1]).then_inc(root_ready, 1)

            def wo_out(l):
                for b in range(4):
                    act.wait_ge(wo_psum[l], b + 1)
                    fn(B[0][:, 2 * b:2 * b + 2], PS[2 + b % 2].rearrange("p (c t) -> p c t", c=2), ACT.Copy)\
                        .then_inc(wo_sbuf[l], 1)
                act.wait_ge(wo_sbuf[l], 4)

            act.wait_ge(x_in, 16)
            act.wait_ge(eps_ready, 1)
            norm(1, XT)
            act.wait_ge(hid_psum, 1)
            fn(HID[:, 0], PS[2][:, 0:TT], ACT.Tanh).then_inc(hid_sbuf, 1)
            act.wait_ge(hid_psum, 2)
            fn(HID[:, 1], PS[3][:, 0:TT], ACT.Copy).then_inc(hid_sbuf, 1)
            act.wait_ge(hid_psum, 3)
            fn(HID[:, 2], PS[4][:, 0:TT], ACT.Sigmoid).then_inc(hid_sbuf, 1)

            def prep_rkv(c, p):
                first = isinstance(c, int) and c == 0
                act.wait_ge(prep_psum, 6 * c + 1)
                if not first:
                    act.wait_ge(prep_pool, 3 * c)
                fn(RKV[:, 0:2], PS[4].rearrange("p (n t) -> p n t", n=2), ACT.Copy)
                act.wait_ge(prep_psum, 6 * c + 2)
                if not first:
                    act.wait_ge(prep_dve, 6 * c)
                    act.wait_ge(z_ready, c - 1)
                fn(RKV[:, 2], PS[5][:, 0:TT], ACT.Copy)
                fn(GATE[p], PS[5][:, TT:2 * TT], ACT.Copy).then_inc(prep_act, 1)

            def prep_tanh(c, p):
                act.wait_ge(prep_psum, 6 * c + 3)
                act.wait_ge(prep_dve, 6 * c + 1)
                for e in range(2):
                    fn(THW[:, e], PS[4 + e][:, 0:TT], ACT.Tanh, scale=0.5, bias=PP[p][:, e:e + 1])
                for e in range(2):
                    last = fn(THA[:, e], PS[4 + e][:, TT:2 * TT], ACT.Tanh, scale=0.5,
                              bias=PP[p][:, 2 + e:3 + e])
                order(last)
                order(fn(LD, THW, ACT.Identity, scale=-0.5 * DECAY, bias=BIASES[:, 2:3]))
                order(fn(THW, THA, ACT.Identity, scale=PP[p][:, 5:6], bias=PP[p][:, 6:7]))
                fn(THA, THA, ACT.Identity, scale=-0.5, bias=BIASES[:, 3:4]).then_inc(prep_act, 1)

            def prep_root(c):
                act.wait_ge(prep_dve, 6 * c + 2)
                fn(ROOT, SQ, ACT.Sqrt).then_inc(prep_act, 1)

            def prep_exp(c):
                act.wait_ge(prep_dve, 6 * c + 4)
                fn(PW, CUM, ACT.Exp)
                act.wait_ge(prep_pool, 3 * c + 2)
                fn(PINV, CUM, ACT.Exp, scale=-1.0)
                fn(PX, CUX, ACT.Exp).then_inc(prep_act, 1)

            def solve(e, c):
                def banks(k):
                    act.wait_ge(chain_psum[e], CH * c + k)
                return banks

            def right_side(e, c):
                act.wait_ge(chain_psum[e], CH * c + 14)
                for hl in range(2):
                    last = fn(RHS[e][:, 2 * hl:2 * hl + 2],
                              PS[2 * e + hl][:, 0:2 * N].rearrange("p (q i) -> p q i", q=2), ACT.Copy)
                last.then_inc(chain_sbuf[e], 1)

            def solve0(e, c):
                act.wait_ge(chain_psum[e], CH * c + 15)
                fn(U[e], PS[2 * e][:, 0:4 * N].rearrange("p (q i) -> p q i", q=4), ACT.Copy)\
                    .then_inc(chain_sbuf[e], 1)

            def solve1(e, c):
                then = slice(64, 128) if e == 0 else slice(0, 64)
                act.wait_ge(chain_psum[e], CH * c + 16)
                fn(WU[e][then], PS[2 * e + 1][then, 0:4 * N].rearrange("p (q i) -> p q i", q=4), ACT.Copy)\
                    .then_inc(chain_sbuf[e], 1)

            def outputs(c):
                act.wait_ge(gn_psum, 3 * c + 1)
                if not (isinstance(c, int) and c == 0):
                    act.wait_ge(state_out, 16 * c)
                fn(SFIN, PS[7][:, TT:TT + 2 * N], ACT.Copy).then_inc(state_ready, 1)
                fn(YT, PS[7][:, 0:TT], ACT.Copy).then_inc(gn_sbuf, 1)
                act.wait_ge(state_ready, c + 1)
                dst = a["out_state"][c] if isinstance(c, int) else \
                    a["out_state"][bass.ds(c, 1)].rearrange("a p n -> (a p) n")
                act.dma_start(dst, SFIN).then_inc(state_out, 16)

            def gn_root_(c):
                act.wait_ge(gn_psum, 3 * c + 3)
                fn(YR, PS[7][:, 0:TT], ACT.Sqrt, bias=BIASES[:, 1:2]).then_inc(gn_root, 1)

            def mix_step(c, prep, tail):
                if tail:
                    gn_root_(c - 1)
                if prep is not None:
                    prep_rkv(*prep)
                    prep_tanh(*prep)
                    prep_root(prep[0])
                    prep_exp(prep[0])
                for f in (right_side, solve0, solve1):
                    for e in range(2):
                        f(e, c)
                outputs(c)

            prep_rkv(0, 0)
            prep_tanh(0, 0)
            prep_root(0)
            prep_exp(0)
            mix_step(0, (1, 1), False)
            with act.Fori(0, 3) as i:
                order.enter(i, STEPS_ACT_MIX)
                mix_step(2 * i + 1, (2 * i + 2, 0), True)
                mix_step(2 * i + 2, (2 * i + 3, 1), True)
                order.leave(3)
            mix_step(7, None, True)
            gn_root_(7)
            wo_out(0)
            norm(2, B[0])
            act.wait_ge(x_ready, 1)
            norm(3, XT)

            with act.Fori(0, 2) as r:
                for k in range(RING):
                    n = RING * r + k
                    act.wait_ge(gu_psum, n + 1)
                    act.wait_ge(hf_ready, n if k == 0 else n - 1)
                    fn(SG[k % 2], PS[k % 2][:, 0:TT], ACT.Silu).then_inc(sg_ready, 1)
            act.wait_ge(yt_psum, 1)
            for b in range(4):
                last = fn(B[0][:, 2 * b:2 * b + 2], PS[2 + b].rearrange("p (c t) -> p c t", c=2), ACT.Copy)
            last.then_inc(yt_sbuf, 1)
            act.wait_ge(yt_sbuf, 1)
            norm(4, B[0])
            act.wait_ge(x_ready, 2)
            norm(5, XT)

            def attend_in(c, p):
                act.wait_ge(qkv_psum, 2 * c + 1)
                if not isinstance(c, int) or c >= 2:
                    half = (c - p) * 8
                    act.wait_ge(kv_out[p], 2 * half)
                    act.wait_ge(att_psum, c - 1)
                fn(QK[p], PS[0].rearrange("p (n t) -> p n t", n=2), ACT.Copy).then_inc(qkv_sbuf, 1)
                act.wait_ge(qkv_psum, 2 * c + 2)
                fn(VA[p], PS[1][:, 0:TT].rearrange("p (g i) -> p g i", g=G), ACT.Copy).then_inc(qkv_sbuf, 1)

            def attend(c, nxt):
                if nxt is not None:
                    attend_in(*nxt)
                act.wait_ge(score_ready, 2 * c + 2)
                if not (isinstance(c, int) and c == 0):
                    act.wait_ge(prob_ready, c)
                for hl in range(2):
                    for s, (lo, hi) in enumerate(((0, P), (P, 3 * P))):
                        last = fn(EX[:, hl, lo:hi], SC[:, hl, lo:hi], ACT.Exp, bias=NMX[:, hl, s:s + 1],
                                  accum_out=SUM[:, hl, s:s + 1])
                last.then_inc(exp_ready, 1)
                act.wait_ge(probT_psum, c + 1)
                if not (isinstance(c, int) and c == 0):
                    act.wait_ge(att_psum, c)
                for hl in range(2):
                    last = fn(PT[:, hl], PS[4 + hl][:, 0:3 * P], ACT.Copy)
                last.then_inc(probT_sbuf, 1)
                act.wait_ge(att_psum, c + 1)
                dst = B[1][:, c] if isinstance(c, int) else B[1][:, bass.ds(c, 1)].rearrange("p a t -> p (a t)")
                fn(dst, PS[6][:, 0:TT], ACT.Copy).then_inc(att_sbuf, 1)

            attend_in(0, 0)
            attend(0, (1, 1))
            with act.Fori(0, 3) as i:
                attend(2 * i + 1, (2 * i + 2, 0))
                attend(2 * i + 2, (2 * i + 3, 1))
            attend(7, None)
            wo_out(1)
            norm(6, B[0])
            act.wait_ge(x_ready, 3)
            norm(7, XT)
            act.wait_ge(hn_psum, 1)
            for b in range(4):
                last = fn(HN[:, b // 2, 512 * (b % 2):512 * (b % 2) + 512], PS[b], ACT.Copy)
            last.then_inc(hn_sbuf, 1)
            act.wait_ge(logit_ready, 1)
            fn(RT["EXL"], RT["LG"], ACT.Exp).then_inc(logit_exp, 1)

            def gathered(j):
                act.wait_ge(gather_psum, j + 1)
                for b in range(2):
                    last = fn(XS[:, 4 * b:4 * b + 4], PS[4 + b].rearrange("p (c s) -> p c s", c=4), ACT.Copy)
                last.then_inc(gather_sbuf, 1)

            def job(j):
                with act.Fori(0, 2) as r:
                    for k in range(RING):
                        n = NF * j + RING * r + k
                        act.wait_ge(egu_psum, n + 1)
                        act.wait_ge(ehf_ready, n if k == 0 else n - 1)
                        fn(SG[k % 2][:, 0:SLOTS], PS[k % 2][:, 0:SLOTS], ACT.Silu).then_inc(esg_ready, 1)
                act.wait_ge(ey_psum, j + 1)
                for half in range(2):
                    last = fn(YSB[:, 512 * half:512 * half + 512], PS[2 + half], ACT.Copy)
                last.then_inc(ey_sbuf, 1)
                gathered(j + 1)

            gathered(0)
            with act.Fori(0, NE) as j:
                job(j)
            act.wait_ge(jobs_ready, 1)
            over = act.value_load(JOBI[0:1, NJ:NJ + 1], min_val=0, max_val=NOVER)
            with act.Fori(0, over) as j:
                job(j + NE)
            act.wait_ge(moe_done, 1)
            norm(8, ACC)

        @block.gpsimd
        def _(pool):
            order = Order(pool, pool_order)
            tt = nc.gpsimd.tensor_tensor

            def prep_keys(c, p):
                pool.wait_ge(prep_act, 4 * c + 1)
                if not (isinstance(c, int) and c == 0):
                    pool.wait_ge(prep_psum, 6 * (c - 1) + 5)
                pool.wait_ge(prep_dve, 6 * c + 1)
                kk = PP[p][:, 4:5].to_broadcast([P, TT])
                order(tt(KKR, RKV[:, 1], kk, ALU.mult))
                tt(SQ, KKR, KKR, ALU.mult).then_inc(prep_pool, 1)

            def prep_shift(c):
                pool.wait_ge(prep_dve, 6 * c + 4)
                tt(CUX, CUM, LD, ALU.subtract).then_inc(prep_pool, 1)

            def prep_factors(c, p):
                first = isinstance(c, int) and c < 2
                pool.wait_ge(prep_act, 4 * c + 4)
                if not first:
                    pool.wait_ge(gn_psum, 3 * (c - 2) + 1)
                if not (isinstance(c, int) and c == 0):
                    pool.wait_ge(prep_psum, 6 * c)
                kin = THW
                for e in range(2):
                    order(tt(kin[:, e], kin[:, e], RKV[:, 1], ALU.mult))
                    order(tt(THA[:, e], THA[:, e], KKN, ALU.mult))
                    tt(AR[p][e][:, 0], KKN, PX[:, e], ALU.mult)
                    tt(AR[p][e][:, 1], RKV[:, 0], PW[:, e], ALU.mult)
                    tt(BT[p][:, e], THA[:, e], PINV[:, e], ALU.mult)
                    order(tt(KT[p][:, e], kin[:, e], PINV[:, e], ALU.mult))
                    end = T - 1 if e == 0 else 0
                    last = PW[:, e, end:end + 1].to_broadcast([P, T])
                    tt(HATT[:, 2 * e], BT[p][:, e, 0:T], last, ALU.mult)
                    order(tt(HATT[:, 2 * e + 1], KT[p][:, e, 0:T], last, ALU.mult))
                order(tt(COEF, kin[:, 0], kin[:, 1], ALU.add))
                order(tt(COEF, COEF, RKV[:, 0], ALU.mult))
                tt(COEF, COEF, PP[p][:, 7:8].to_broadcast([P, TT]), ALU.mult).then_inc(prep_pool, 1)

            def prep(c, p):
                prep_keys(c, p)
                prep_shift(c)
                prep_factors(c, p)

            prep(0, 0)
            prep(1, 1)
            with pool.Fori(0, 3) as i:
                order.enter(i, STEPS_POOL_MIX)
                prep(2 * i + 2, 0)
                prep(2 * i + 3, 1)
                order.leave(3)

            pool.wait_ge(h_ready, 3)
            for p in range(2):
                nc.gpsimd.memset(BIAS[p][:, :, 0:P], 0.0)
                order(nc.gpsimd.memset(BIAS[p][:, :, 2 * P:3 * P], 0.0))

            def bias(c, r, p):
                pool.wait_ge(apair_full[p], 16 * (r + 1))
                if not isinstance(c, int) or c >= 2:
                    pool.wait_ge(score_ready, 2 * (c - 1))
                raw = W[:, HALF * p + BLK:HALF * p + BLK + 2 * P].rearrange("p (h k) -> p h k", h=2)
                tt(BIAS[p][:, :, P:2 * P], raw, con("window").unsqueeze(1).to_broadcast([P, 2, P]), ALU.add)\
                    .then_inc(bias_ready, 1)

            def leave(c, p):
                pool.wait_ge(qkv_sbuf, 2 * c + 2)
                for name, src in (("out_k", QK[p][:, 1, 0:T]), ("out_v", VA[p][:, 0])):
                    dst = a[name][c] if isinstance(c, int) else a[name][bass.ds(c, 1)].rearrange("a p n -> (a p) n")
                    pool.dma_start(dst, src).then_inc(kv_out[p], 16)

            for c in range(2):
                bias(c, 0, c)
                leave(c, c)
            with pool.Fori(0, 3) as i:
                for p in range(2):
                    bias(2 * i + 2 + p, i + 1, p)
                    leave(2 * i + 2 + p, p)

        @block.vector
        def _(dve):
            order = Order(dve, dve_order)
            tt, ts, stt = nc.vector.tensor_tensor, nc.vector.tensor_scalar, nc.vector.scalar_tensor_tensor
            nc.vector.memset(BIASES[:, 0:1], RMS_EPS)
            nc.vector.memset(BIASES[:, 2:3], -0.5 * DECAY)
            nc.vector.memset(BIASES[:, 3:4], -0.5)
            nc.vector.memset(BIASES[:, 1:2], GN_EPS).then_inc(eps_ready, 1)
            nc.vector.memset(ZERO, 0.0).then_inc(zero_ready, 1)

            def gains(l):
                dve.wait_ge(col_in, 16)
                dve.wait_ge(mod_used[l], 16)
                b = col(f"mod_b{l}").unsqueeze(2).to_broadcast([P, 6 * C, G])
                order(tt(MOD[:, l], PS[0][:, 0:12 * C].rearrange("p (j g) -> p j g", g=G), b, ALU.add))
                for n, (name, at, add) in enumerate((("pre_mix", 1, 1.0), ("post_mix", 2, 0.0), ("pre_ffn", 4, 1.0),
                                                     ("post_ffn", 5, 0.0))):
                    g = col(f"{name}{l}").unsqueeze(2).to_broadcast([P, C, G])
                    last = stt(GAIN[:, l, n], MOD[:, l, C * at:C * at + C], add, g, ALU.add, ALU.mult)
                last.then_inc(mod_ready, 1)
                dve.wait_ge(mod_ready, l + 1)

            def norm_pre(n, l, k):
                dve.wait_ge(root_ready, n)
                order(nc.vector.reciprocal(RSTD, RMS))
                order(tt(B[1], XT, RSTD.unsqueeze(1).to_broadcast([P, C, TT]), ALU.mult))
                for c in range(C):
                    for g in range(G):
                        cs = slice(T * g, T * g + T)
                        last = ts(HT[:, c, cs], B[1][:, c, cs], GAIN[:, l, k, c, g:g + 1],
                                  MOD[:, l, (0 if k == 0 else 3) * C + c, g:g + 1], ALU.mult, ALU.add)
                last.then_inc(h_ready, 1)

            def norm_post(n, l, k, src, order=order):
                dve.wait_ge(root_ready, n)
                order(nc.vector.reciprocal(RSTD, RMS))
                order(tt(B[1], src, RSTD.unsqueeze(1).to_broadcast([P, C, TT]), ALU.mult))
                for c in range(C):
                    for g in range(G):
                        cs = slice(T * g, T * g + T)
                        last = stt(XT[:, c, cs], B[1][:, c, cs], GAIN[:, l, k, c, g:g + 1], XT[:, c, cs],
                                   ALU.mult, ALU.add)
                last.then_inc(x_ready, 1)

            gains(0)
            for n, (name, at, f, b) in enumerate((("w0", 0, 0.5, 0.0), ("w0", C, 0.5, 0.0), ("a0", 0, 0.5, 0.0),
                                                  ("a0", C, 0.5, 0.0), ("k_k", 0, 1.0, 0.0), ("k_a", 0, 0.5, 0.0),
                                                  ("k_a", 0, -0.5, 1.0), ("r_k", 0, 1.0, 0.0),
                                                  ("lnx_w", 0, 1.0, 0.0), ("lnx_b", 0, 1.0, 0.0))):
                last = ts(PAIR[:, :, n], col(name)[:, at:at + C], f, b, ALU.mult, ALU.add)
            order(last)
            norm_pre(1, 0, 0)
            dve.wait_ge(h_ready, 1)
            hh = HT.rearrange("p c (g t) -> p (c g) t", g=G)
            xx = XX.rearrange("p (n t) -> p n t", t=T)
            tt(xx[:, :, 1:T - 1], hh[:, :, 0:T - 2], hh[:, :, 2:T], ALU.add)
            nc.vector.tensor_copy(xx[:, :, 0:1], hh[:, :, 1:2])
            order(nc.vector.tensor_copy(xx[:, :, T - 1:T], hh[:, :, T - 2:T - 1]))
            order(stt(xx, xx, 0.5, hh, ALU.mult, ALU.subtract))
            xc = XX.rearrange("p (c t) -> p c t", c=C)
            for n, v in enumerate((1, 4, 5, 0, 2, 3)):
                if n >= 3:
                    dve.wait_ge(hid_psum, n - 2)
                for c in range(C):
                    last = stt(B[n % 3][:, c], xc[:, c], col("mu")[:, C * v + c:C * v + c + 1], HT[:, c],
                               ALU.mult, ALU.add)
                last.then_inc(mixed_ready, 1)
            dve.wait_ge(mixed_ready, 6)
            dve.wait_ge(s0_in, 16)
            s0 = STATE0.rearrange("p (c e i) -> p c e i", c=C, e=2)

            def prep_params(c, p):
                if not isinstance(c, int) or c >= 2:
                    dve.wait_ge(z_ready, c - 1)
                cs = slice(c, c + 1) if isinstance(c, int) else bass.ds(c, 1)
                ts(S0P[p].unsqueeze(1), s0[:, cs], float(np.exp(-CENTRE)), None, ALU.mult)
                nc.vector.tensor_copy(PP[p].unsqueeze(1), PAIR[:, cs]).then_inc(prep_dve, 1)

            def prep_floor(c):
                dve.wait_ge(prep_psum, 6 * c + 4)
                ts(SQ, PS[6][:, 0:TT], 1e-24, None, ALU.max).then_inc(prep_dve, 1)

            def prep_unit(c):
                dve.wait_ge(prep_act, 4 * c + 3)
                order(nc.vector.reciprocal(RROOT, ROOT))
                stt(KKN, KKR, -1.0, RROOT, ALU.mult, ALU.mult).then_inc(prep_dve, 1)

            def prep_scan(c):
                dve.wait_ge(prep_act, 4 * c + 2)
                for e in range(2):
                    for g in range(G):
                        cs = slice(T * g, T * g + T)
                        x, y = LD[:, e, cs], CUM[:, e, cs]
                        if e:
                            x, y = x[:, ::-1], y[:, ::-1]
                        last = nc.vector.tensor_tensor_scan(y, ONES, x, CENTRE, ALU.mult, ALU.add)
                last.then_inc(prep_dve, 1)

            def prep_bonus(c, p):
                dve.wait_ge(prep_psum, 6 * c + 5)
                tt(BONUS[p], PS[6][:, 0:TT], RKV[:, 2], ALU.mult)
                nc.vector.tensor_copy(VN[p], PS[6][:, TT:2 * TT].rearrange("p (g i) -> p g i", g=G))\
                    .then_inc(prep_dve, 1)

            def prep_hat(c, p):
                dve.wait_ge(prep_psum, 6 * c + 6)
                nc.vector.tensor_copy(HATN[p], PS[6].rearrange("p (n j) -> p n j", n=4)).then_inc(prep_dve, 1)

            def gram(e, c, k):
                dve.wait_ge(chain_psum[e], CH * c + k)
                if k < 3:
                    dst = (GB if k == 1 else GK)[e]
                    m = SEEN[:, e].rearrange("p k t -> p (k t)").unsqueeze(1).to_broadcast([P, 2, 2 * P])
                    for hl in range(2):
                        last = tt(dst[:, 2 * hl:2 * hl + 2].rearrange("p q k t -> p q (k t)"),
                                  PS[2 * e + hl].rearrange("p (q x) -> p q x", q=2), m, ALU.mult)
                    last.then_inc(chain_sbuf[e], 1)
                    return
                for hl in range(2):
                    tt(TN[e][:, 2 * hl:2 * hl + 2], PS[2 * e + hl][:, 0:2 * P].rearrange("p (q t) -> p q t", q=2),
                       PAIRM[:, e].unsqueeze(1).to_broadcast([P, 2, P]), ALU.mult)
                order(tt(TR[e], GB[e][:, :, 0], PAIRT[:, e].unsqueeze(1).to_broadcast([P, 4, P]), ALU.mult))
                eye = IDENT.unsqueeze(1).to_broadcast([P, 4, P])
                tt(TN[e], TN[e], eye, ALU.add)
                tt(TR[e], TR[e], eye, ALU.add).then_inc(chain_sbuf[e], 1)

            def level_z(e, c, n):
                dve.wait_ge(chain_psum[e], CH * c + 2 * n + 2)
                tt(Z[e], PS[2 * e].rearrange("p (q t) -> p q t", q=4),
                   LEVEL[:, e, n - 1].unsqueeze(1).to_broadcast([P, 4, P]), ALU.mult).then_inc(chain_sbuf[e], 1)

            def level_d(e, c, n):
                dve.wait_ge(chain_psum[e], CH * c + 2 * n + 3)
                if n < 5:
                    tt(TN[e], TN[e], PS[2 * e + 1].rearrange("p (q t) -> p q t", q=4), ALU.add)
                tt(TR[e], TR[e], PS[2 * e].rearrange("p (q t) -> p q t", q=4), ALU.add).then_inc(chain_sbuf[e], 1)

            def solve2(e, c):
                then = slice(64, 128) if e == 0 else slice(0, 64)
                dve.wait_ge(chain_psum[e], CH * c + 17)
                tt(U[e][then], U[e][then], PS[2 * e][then, 0:4 * N].rearrange("p (q i) -> p q i", q=4), ALU.add)\
                    .then_inc(chain_sbuf[e], 1)

            def gn_centre(c):
                dve.wait_ge(gn_psum, 3 * c + 2)
                order(tt(YC, YT, PS[7][:, 0:TT], ALU.subtract))
                tt(YQ, YC, YC, ALU.mult).then_inc(gn_sbuf, 1)

            def gn_tail(c, p):
                dve.wait_ge(gn_root, c + 1)
                order(nc.vector.reciprocal(YS, YR))
                order(tt(YS, YC, YS, ALU.mult))
                order(ts(YS, YS, PP[p][:, 8:9], PP[p][:, 9:10], ALU.mult, ALU.add))
                order(tt(YS, YS, BONUS[p], ALU.add))
                dst = HT[:, c] if isinstance(c, int) else HT[:, bass.ds(c, 1)].rearrange("p a t -> p (a t)")
                tt(dst, YS, GATE[p], ALU.mult).then_inc(z_ready, 1)

            def mix_step(c, p, prep, tail):
                for e in range(2):
                    gram(e, c, 1)
                if tail:
                    gn_centre(c - 1)
                if tail:
                    gn_tail(c - 1, 1 - p)
                if prep is not None:
                    prep_params(*prep)
                for e in range(2):
                    gram(e, c, 2)
                for e in range(2):
                    gram(e, c, 3)
                if prep is not None:
                    prep_floor(prep[0])
                for n in range(1, 6):
                    for e in range(2):
                        level_z(e, c, n)
                    for e in range(2):
                        level_d(e, c, n)
                    if prep is not None and n == 1:
                        prep_unit(prep[0])
                        prep_scan(prep[0])
                    if prep is not None and n == 4:
                        prep_bonus(*prep)
                if prep is not None:
                    prep_hat(*prep)
                for e in range(2):
                    solve2(e, c)

            prep_params(0, 0)
            prep_floor(0)
            prep_unit(0)
            prep_scan(0)
            prep_bonus(0, 0)
            prep_hat(0, 0)
            mix_step(0, 0, (1, 1), False)
            with dve.Fori(0, 3) as i:
                order.enter(i, STEPS_DVE_MIX)
                mix_step(2 * i + 1, 1, (2 * i + 2, 0), True)
                mix_step(2 * i + 2, 0, (2 * i + 3, 1), True)
                order.leave(3)
            mix_step(7, 1, None, True)
            gn_centre(7)
            gn_tail(7, 1)
            norm_post(2, 0, 1, B[0])
            norm_pre(3, 0, 2)

            with dve.Fori(0, 2) as r:
                for k in range(RING):
                    n = RING * r + k
                    dve.wait_ge(sg_ready, n + 1)
                    dve.wait_ge(ffn_used, n if k == 0 else n - 1)
                    tt(HF[k % 2], SG[k % 2], PS[k % 2][:, TT:2 * TT], ALU.mult).then_inc(hf_ready, 1)
            gains(1)
            norm_post(4, 0, 3, B[0])
            norm_pre(5, 1, 0)

            def attend(c, p):
                dve.wait_ge(score_psum, c + 1)
                dve.wait_ge(bias_ready, c + 1)
                if not (isinstance(c, int) and c == 0):
                    dve.wait_ge(exp_ready, c)
                for hl in range(2):
                    last = stt(SC[:, hl], PS[2 + hl][:, 0:3 * P], SCALE, BIAS[p][:, hl], ALU.mult, ALU.add)
                last.then_inc(score_ready, 1)
                dve.wait_ge(score_ready, 2 * c + 1)
                nc.vector.reduce_max(MX[:, :, 0:1], SC[:, :, 0:P], AX)
                order(nc.vector.reduce_max(MX[:, :, 1:2], SC[:, :, P:3 * P], AX))
                ts(NMX, MX, -1.0, None, ALU.mult).then_inc(score_ready, 1)
                dve.wait_ge(exp_ready, c + 1)
                order(nc.vector.reciprocal(RSUM, SUM))
                if not (isinstance(c, int) and c == 0):
                    dve.wait_ge(probT_psum, c)
                for hl in range(2):
                    for s, (lo, hi) in enumerate(((0, P), (P, 3 * P))):
                        last = ts(PN[:, hl, lo:hi], EX[:, hl, lo:hi], RSUM[:, hl, s:s + 1], None, ALU.mult)
                last.then_inc(prob_ready, 1)

            attend(0, 0)
            with dve.Fori(0, 3) as i:
                order.enter(i, STEPS_DVE_ATT)
                attend(2 * i + 1, 1)
                attend(2 * i + 2, 0)
                order.leave(3)
            attend(7, 1)
            norm_post(6, 1, 1, B[0])
            norm_pre(7, 1, 2)

            lg, ex, pr, ra, oh1, pr2, oh2, chs, wt, pm = (RT[n] for n in names)

            def wide(x):
                return x.unsqueeze(2).to_broadcast([P, G, NE])

            def both(x):
                return x.unsqueeze(1).to_broadcast([P, G, NE])

            dve.wait_ge(logit_psum, 1)
            order(tt(lg, PS[4][:, 0:G * NE].rearrange("p (g e) -> p g e", g=G), both(col("router_b")), ALU.add))
            order(nc.vector.reduce_max(R2[0], lg, AX))
            tt(lg, lg, wide(R2[0]), ALU.subtract).then_inc(logit_ready, 1)
            dve.wait_ge(logit_exp, 1)
            order(nc.vector.reduce_sum(R2[1], ex, AX))
            order(nc.vector.reciprocal(R2[2], R2[1]))
            order(tt(pr, ex, wide(R2[2]), ALU.mult))

            def first_largest(out, x, m, v):
                order(nc.vector.reduce_max(m, x, AX))
                order(tt(ra, x, wide(m), ALU.is_equal))
                order(tt(ra, ra, both(con("expert_rank")), ALU.mult))
                order(nc.vector.reduce_max(v, ra, AX))
                order(tt(out, ra, wide(v), ALU.is_equal))

            first_largest(oh1, pr, R2[3], R2[4])
            order(stt(pr2, oh1, -2.0, pr, ALU.mult, ALU.add))
            first_largest(oh2, pr2, R2[3], R2[4])
            order(tt(chs, oh1, oh2, ALU.add))
            tt(wt, pr, chs, ALU.mult).then_inc(chosen, 1)
            dve.wait_ge(chosen, 1)
            order(nc.vector.reduce_sum(R2[5], wt, AX))
            order(nc.vector.reciprocal(R2[6], R2[5]))
            nc.vector.memset(JOBP, -1.0)
            nc.vector.memset(JOBW, 0.0)
            order(nc.vector.memset(JOBE, 0.0))
            order(tt(JOBW[:, :, 0:NE], wt, wide(R2[6]), ALU.mult))
            dve.wait_ge(place_psum, 1)
            order(tt(pm, PS[5][:, 0:G * NE].rearrange("p (g e) -> p g e", g=G), chs, ALU.mult))
            order(ts(ra, chs, -1.0, 1e6, ALU.add, ALU.mult))
            order(tt(pm, pm, ra, ALU.add))
            nc.vector.tensor_copy(JOBP[:, :, 0:NE], pm)
            order(ts(CNT[:, 0], PS[5][:, 2 * NE:3 * NE], SLOTS + 0.5, None, ALU.is_gt))
            order(nc.vector.tensor_tensor_scan(CNT[:, 1], ONES[:, 0:NE], CNT[:, 0], 0.0, ALU.mult, ALU.add))
            order(tt(CNT[:, 2], CNT[:, 1], CNT[:, 0], ALU.subtract))
            order(ts(pm, pm, -float(SLOTS), None, ALU.add))
            for k in range(NOVER):
                order(stt(CNT[:, 3], CNT[:, 2], float(k), CNT[:, 0], ALU.is_equal, ALU.mult))
                order(tt(JT, both(CNT[:, 3]), pm, ALU.mult))
                order(nc.vector.reduce_sum(JOBP[:, :, NE + k:NE + k + 1], JT, AX))
                order(tt(JT, both(CNT[:, 3]), JOBW[:, :, 0:NE], ALU.mult))
                order(nc.vector.reduce_sum(JOBW[:, :, NE + k:NE + k + 1], JT, AX))
                order(tt(CNT[:, 3], CNT[:, 3], con("expert"), ALU.mult))
                order(nc.vector.reduce_sum(JOBE[:, NE + k:NE + k + 1], CNT[:, 3], AX))
            nc.vector.tensor_copy(JOBI[:, 0:NJ], JOBE)
            nc.vector.tensor_copy(JOBI[:, NJ:NJ + 1], CNT[:, 1, NE - 1:NE]).then_inc(jobs_ready, 1)

            def select(j):
                js = slice(j, j + 1) if isinstance(j, int) else bass.ds(j, 1)
                for g in range(G):
                    last = ts(SEL[:, g], con("slot"), JOBP[:, g, js], None, ALU.is_equal)
                order(last)
                for g in range(G):
                    last = ts(SELW[:, g], SEL[:, g], JOBW[:, g, js], None, ALU.mult)
                last.then_inc(sel_ready, 1)

            def weights_turned(j):
                dve.wait_ge(selT_psum, j + 1)
                nc.vector.tensor_copy(SELWT, PS[0][:, 0:TT]).then_inc(selT_sbuf, 1)

            def job(j):
                select(j + 1)
                with dve.Fori(0, 2) as r:
                    for k in range(RING):
                        n = NF * j + RING * r + k
                        dve.wait_ge(esg_ready, n + 1)
                        dve.wait_ge(exp_used, n if k == 0 else n - 1)
                        tt(HF[k % 2][:, 0:SLOTS], SG[k % 2][:, 0:SLOTS], PS[k % 2][:, SLOTS:2 * SLOTS], ALU.mult)\
                            .then_inc(ehf_ready, 1)
                for b in range(4):
                    dve.wait_ge(scat_psum, 4 * j + b + 1)
                    part = ACC[:, 2 * b:2 * b + 2]
                    tt(part, part, PS[(6, 7, 4, 5)[b]].rearrange("p (c t) -> p c t", c=2), ALU.add)\
                        .then_inc(scat_acc, 1)
                weights_turned(j + 1)

            order(nc.vector.memset(ACC, 0.0))
            select(0)
            weights_turned(0)
            with dve.Fori(0, NE) as j:
                order.enter(j, STEPS_DVE_JOB)
                job(j)
                order.leave(NE)
            over = dve.value_load(JOBI[0:1, NJ:NJ + 1], min_val=0, max_val=NOVER)
            with dve.Fori(0, over) as j:
                order.enter(j, STEPS_DVE_JOB)
                job(j + NE)
            nc.vector.memset(RT["LG"], 0.0).then_inc(moe_done, 1)
            norm_post(8, 1, 3, ACC, Order(dve, last_order))


def pack(x):
    f = {n: np.asarray(v) for n, v in x.items()}

    def cols(v):
        v = v.reshape(-1, C, P)
        return v.transpose(2, 0, 1).reshape(P, -1)

    def tiles(w):
        k, m = w.shape
        return w.reshape(k // P, P, m // P, P).transpose(1, 2, 0, 3)

    c = {}
    for l in range(2):
        for n in ("mix_pre", "mix_post", "ffn_pre", "ffn_post"):
            kind, when = n.split("_")
            c[f"{when}_{kind}{l}"] = cols(f[f"l{l}_norm_{n}"])
        c[f"mod_b{l}"] = cols(f[f"l{l}_mod_b"])
    for n in ("mu", "w0", "a0", "k_k", "k_a", "lnx_w", "lnx_b"):
        c[n] = cols(f["l0_" + n])
    c["r_k"] = cols(f["l0_r_k"].reshape(D))
    c["cond"] = np.stack([f["c_ctx"], f["c"][0]], 1).reshape(C, P, G).transpose(1, 0, 2).reshape(P, -1)
    c["router_w"] = f["l1_router_w"].reshape(C, P, NE).transpose(1, 0, 2).reshape(P, -1)
    c["router_b"] = np.broadcast_to(f["l1_router_b"], (P, NE))
    out = {"cols": np.concatenate([c[n] for n in COLS], 1)}
    out["cons"] = shape_constants()
    tok = np.concatenate([f["x_prompt"][0], f["x_sample"][0]], 0)
    out["x"] = tok.reshape(TT, C, P).transpose(2, 1, 0)
    s0 = f["state_l0"][0].reshape(2, C, 2, N, N)
    out["state0"] = s0.transpose(2, 4, 1, 0, 3).reshape(P, -1)
    out["w_mod"] = np.stack([tiles(f[f"l{l}_mod_w"]).reshape(P, 16, BLK).transpose(1, 0, 2) for l in range(2)])
    e1 = [f[n].transpose(1, 0, 2).reshape(D, P) for n in ("l0_w1", "l0_a1")] + [f["l0_g1"]]
    out["w_lora"] = np.concatenate([tiles(w).reshape(P, D) for w in e1], 1)
    rkv = [tiles(f["l0_" + n]) for n in ("wr", "wk", "wv")]
    e2 = [f[n].reshape(P, C, P) for n in ("l0_w2", "l0_a2", "l0_g2")]
    out["w_rkv"] = np.stack([np.concatenate([w[:, j].reshape(P, D) for w in rkv] + [w[:, j] for w in e2], 1)
                             for j in range(C)])
    out["w_o"] = np.stack([tiles(f[f"l{l}_wo"]).reshape(P, C * D) for l in range(2)])

    def swiglu(wg, wu, wd):
        g, u = tiles(wg), tiles(wu)
        return np.stack([np.concatenate([g[:, j].reshape(P, D), u[:, j].reshape(P, D), wd[P * j:P * j + P]], 1)
                         for j in range(NF)])

    out["w_ffn"] = swiglu(f["l0_ffn_wg"], f["l0_ffn_wu"], f["l0_ffn_wd"])
    out["w_exp"] = np.stack([swiglu(f["l1_exp_wg"][e], f["l1_exp_wu"][e], f["l1_exp_wd"][e]) for e in range(NE)])
    tq, tk = np.arange(T)[:, None], np.arange(T)[None]
    ridx = tk // GRID_W - tq // GRID_W + 7
    cidx = np.clip(tk % GRID_W - tq % GRID_W + WIN_W - 1, 0, 2 * WIN_W - 2)
    rel = f["l1_rpb"][:, ridx, cidx].reshape(C, 2, T, T).transpose(0, 2, 1, 3).reshape(C, T, 2 * T)
    ck = f["cache_k_l1"][0].reshape(C, 2, T, N).transpose(0, 1, 3, 2).reshape(C, P, T)
    cv = f["cache_v_l1"][0].reshape(C, 2, T, N).transpose(0, 2, 1, 3).reshape(C, T, P)
    w = tiles(f["l1_wqkv"])
    out["w_qkv"] = np.stack([np.concatenate([w[:, C * n + j].reshape(P, D) for n in range(3)]
                                            + [rel[j], ck[j], cv[j]], 1) for j in range(C)])
    return {n: np.ascontiguousarray(v) for n, v in out.items()}


_OUTS = {"out_x": (P, C, TT), "out_state": (C, P, 2 * N), "out_k": (C, P, T), "out_v": (C, T, P)}


def unpack(r):
    x = r["out_x"].transpose(2, 1, 0).reshape(TT, D)
    s = r["out_state"].reshape(C, 2, N, 2, N).transpose(3, 0, 1, 2, 4).reshape(1, 2, H, N, N)
    k = r["out_k"].reshape(C, 2, N, T).transpose(0, 1, 3, 2).reshape(1, H, T, N)
    v = r["out_v"].reshape(C, T, 2, N).transpose(0, 2, 1, 3).reshape(1, H, T, N)
    return tuple(np.ascontiguousarray(o) for o in (x[None, 0:T], x[None, T:], s, k, v))


def kernel(**inputs):
    import concourse.bacc as _bacc
    from concourse import mybir as _mybir
    from concourse.bass_utils import run_bass_kernel_spmd as _run

    nc = _bacc.Bacc("TRN2", target_bir_lowering=False, num_devices=1)
    arrays = pack(inputs)
    aps = {n: nc.dram_tensor(n, v.shape, _mybir.dt.from_np(v.dtype), kind="ExternalInput").ap()
           for n, v in arrays.items()}
    for n, shape in _OUTS.items():
        aps[n] = nc.dram_tensor(n, shape, _mybir.dt.float32, kind="ExternalOutput").ap()
    build(nc, aps)
    r = _run(nc, [arrays], core_ids=[0])
    return unpack(r.results[0])
```

```python
from contextlib import ExitStack

import concourse.bass as bass
import numpy as np
from concourse import mybir

F32 = mybir.dt.float32
F32R = mybir.dt.float32r
I32 = mybir.dt.int32
ALU = mybir.AluOpType
ACT = mybir.ActivationFunctionType
AX = mybir.AxisListType.X

P = 128
D = 1024
H = 16
N = D // H
T = 128
G = 2
TT = G * T
C = D // P
FF = 2816
FB = 2 * P
NS = FF // FB
NE = 8
GRID_W, WIN_W = 64, 16
RMS_EPS, GN_EPS = 1e-6, 64e-5
SCALE = N ** -0.5
SLOTS = P
NOVER = (TT * 2) // (SLOTS + 1)
NJ = NE + NOVER + 1
DECAY = float(np.exp(-0.5))
CENTRE = 0.5 * T * DECAY

RING = 11
LOAD = 2048
UNIT = 1024
NBUF = 3
FFN_LOADS = 3 * NS
MOD_LOADS = 6 * D * C // LOAD
MOD_TILES = 6 * D // 512
BLK = 3 * D
HALF = BLK + 512
W_COLS = 25600
EXTRA = 1536
START = {"mod0": 0, "ffn": 3, "mod1": 3, "exp": 3}
UNITS = {"mod0": 0, "ffn": 2 * MOD_LOADS, "mod1": 2 * (MOD_LOADS + FFN_LOADS),
         "exp": 2 * (2 * MOD_LOADS + FFN_LOADS)}

COLS = {}
_at = 0
for _n, _w in [("pre_mix0", C), ("post_mix0", C), ("pre_ffn0", C), ("post_ffn0", C),
               ("pre_mix1", C), ("post_mix1", C), ("pre_ffn1", C), ("post_ffn1", C),
               ("mu", 6 * C), ("w0", 2 * C), ("a0", 2 * C), ("k_k", C), ("k_a", C), ("r_k", C),
               ("lnx_w", C), ("lnx_b", C), ("mod_b0", 6 * C), ("mod_b1", 6 * C), ("cond", 2 * C),
               ("router_w", NE * C), ("router_b", NE)]:
    COLS[_n] = (_at, _w)
    _at += _w
NCOLS = _at
KCON = {}
_at = 0
for _n, _w in [("ident", P), ("ones", P), ("heads", P),
               ("seen", 2 * 2 * P), ("pair", 2 * P), ("level", 2 * 5 * P),
               ("window", P), ("slot", P), ("expert", NE), ("expert_rank", NE),
               ("join", G)]:
    KCON[_n] = (_at, _w)
    _at += _w
NCON = _at


def shape_constants():
    s, t = np.arange(P)[:, None], np.arange(P)[None]
    k = {"ident": s == t, "ones": s + t >= 0, "heads": s // N == t // N}
    k["seen"] = np.stack([s < t, s <= t, s > t, s >= t], 1)

    def off(b, lower):
        same = s // (2 * b) == t // (2 * b)
        odd, even = (s // b) % 2 == 1, (t // b) % 2 == 0
        return same & ((odd & even) if lower else (~odd & ~even))

    k["pair"] = np.stack([off(1, True), off(1, False)], 1)
    k["level"] = np.stack([off(2 ** n, low) for low in (True, False) for n in range(1, 6)], 1)
    qc, kc = s % GRID_W, t % GRID_W
    ws = np.clip(qc - WIN_W // 2, 0, GRID_W - WIN_W)
    k["window"] = np.where((kc >= ws) & (kc < ws + WIN_W), 0.0, -1e30)
    k["slot"] = t + 0 * s
    k["expert"] = np.arange(NE)[None] + 0 * s
    k["expert_rank"] = NE - np.arange(NE)[None] + 0 * s
    k["join"] = s % G == np.arange(G)[None]
    return np.concatenate([np.asarray(k[n], np.float32).reshape(P, w) for n, (_, w) in KCON.items()], 1)


class Order:

    def __init__(self, eng, sem):
        self.eng, self.sem, self.before, self.n, self.lead = eng, sem, 0, 0, 0

    def __call__(self, ins):
        ins.then_inc(self.sem, 1)
        self.n += 1
        self.eng.wait_ge(self.sem, self.lead + self.n)

    def enter(self, i, per):
        self.before, self.n, self.per = self.before + self.n, 0, per
        self.lead = self.before + i * per

    def leave(self, turns):
        if self.n != self.per:
            raise ValueError(f"the loop has {self.n} steps, not {self.per}")
        self.before += turns * self.per
        self.n, self.lead = 0, self.before


STEPS_DVE_MIX = 16
STEPS_ACT_MIX = 6
STEPS_POOL_MIX = 22
STEPS_DVE_ATT = 4
STEPS_DVE_JOB = 1


def build(nc, a):
    with ExitStack() as ctx:
        def sb(name, cols, dt=F32):
            return ctx.enter_context(nc.sbuf_tensor(name, [P, cols], dt))[:, :]

        def sem(name):
            return ctx.enter_context(nc.semaphore(name))

        W = sb("W", W_COLS)
        XT = sb("XT", C * TT).rearrange("p (c t) -> p c t", c=C)
        HT = sb("HT", C * TT).rearrange("p (c t) -> p c t", c=C)
        B = [sb(f"B{i}", C * TT).rearrange("p (c t) -> p c t", c=C) for i in range(3)]
        COL = sb("COL", NCOLS)
        CON = sb("CON", NCON)
        HI = sb("HI", NBUF * UNIT, F32R).rearrange("p (n x) -> p n x", n=NBUF)
        LO = sb("LO", NBUF * UNIT, F32R).rearrange("p (n x) -> p n x", n=NBUF)
        XHI = sb("XHI", C * TT, F32R).rearrange("p (c t) -> p c t", c=C)
        XLO = sb("XLO", C * TT, F32R).rearrange("p (c t) -> p c t", c=C)
        HHI = sb("HHI", 2 * TT, F32R).rearrange("p (f t) -> p f t", f=2)
        HLO = sb("HLO", 2 * TT, F32R).rearrange("p (f t) -> p f t", f=2)
        MOD = sb("MOD", 2 * 6 * C * G).rearrange("p (l j g) -> p l j g", l=2, g=G)
        COND = sb("COND", C * G).rearrange("p (c g) -> p c g", g=G)
        GAIN = sb("GAIN", 4 * 2 * C * G).rearrange("p (l k c g) -> p l k c g", l=2, k=4, g=G)
        RMS = sb("RMS", TT)
        RSTD = RMS
        BIASES = sb("BIASES", 4)
        HID = sb("HID", 3 * TT).rearrange("p (n t) -> p n t", n=3)
        PAIR = sb("PAIR", C * 10).rearrange("p (c n) -> p c n", n=10)
        PS = [ctx.enter_context(nc.psum_tensor(f"PS{i}", [P, 512], F32))[:, :] for i in range(8)]

        def col(name):
            at, w = COLS[name]
            return COL[:, at:at + w]

        def con(name):
            at, w = KCON[name]
            return CON[:, at:at + w]

        IDENT, ONES, HEADS = con("ident"), con("ones"), con("heads")
        SEEN = con("seen").rearrange("p (e k t) -> p e k t", e=2, k=2)
        PAIRM = con("pair").rearrange("p (e t) -> p e t", e=2)
        PAIRT = PAIRM[:, ::-1]
        LEVEL = con("level").rearrange("p (e n t) -> p e n t", e=2, n=5)

        def raw_unit(phase, u):
            at = (START[phase] + u // 2) % RING * LOAD + u % 2 * UNIT
            return W[:, at:at + UNIT]

        extra = sb("extra", EXTRA)
        areas = {}
        WO1 = W_COLS - C * D

        def scratch(phase, cols):
            at = areas.setdefault(phase, [2 * HALF, 0])
            if at[0] + cols <= (W_COLS if phase == 0 else WO1):
                at[0] += cols
                return W[:, at[0] - cols:at[0]]
            at[1] += cols
            if at[1] > EXTRA:
                raise ValueError(f"phase {phase} needs {at[1]} floats")
            return extra[:, at[1] - cols:at[1]]

        def two(ap):
            return ap.rearrange("p (e t) -> p e t", e=2)

        AR = [[scratch(0, 2 * TT).rearrange("p (k t) -> p k t", k=2) for _ in range(2)] for _ in range(2)]
        BT = [two(scratch(0, 2 * TT))] * 2
        KT = [two(scratch(0, 2 * TT))] * 2
        GATE = [scratch(0, TT) for _ in range(2)]
        BONUS = [scratch(0, TT) for _ in range(2)]
        VN = [scratch(0, TT).rearrange("p (g i) -> p g i", g=G) for _ in range(2)]
        HATN = [scratch(0, 4 * P).rearrange("p (n j) -> p n j", n=4) for _ in range(2)]
        S0P = [scratch(0, 2 * N).rearrange("p (e i) -> p e i", e=2) for _ in range(2)]
        PP = [scratch(0, 10) for _ in range(2)]
        RKV = scratch(0, 3 * TT).rearrange("p (n t) -> p n t", n=3)
        KKR = scratch(0, TT)
        SQ = scratch(0, TT)
        KKN, ROOT, RROOT, COEF = KKR, SQ, SQ, SQ
        THW = two(scratch(0, 2 * TT))
        THA = two(scratch(0, 2 * TT))
        LD = two(scratch(0, 2 * TT))
        CUM = two(scratch(0, 2 * TT))
        CUX = two(scratch(0, 2 * TT))
        PW = two(scratch(0, 2 * TT))
        PINV, PX = CUM, CUX
        HATT = LD.rearrange("p e t -> p (e t)").rearrange("p (n t) -> p n t", n=4)
        GB = [scratch(0, 8 * P).rearrange("p (q k t) -> p q k t", q=4, k=2) for _ in range(2)]
        GK = [scratch(0, 8 * P).rearrange("p (q k t) -> p q k t", q=4, k=2) for _ in range(2)]
        TN = [scratch(0, 4 * P).rearrange("p (q t) -> p q t", q=4) for _ in range(2)]
        TR = [scratch(0, 4 * P).rearrange("p (q t) -> p q t", q=4) for _ in range(2)]
        Z = [scratch(0, 4 * P).rearrange("p (q t) -> p q t", q=4) for _ in range(2)]
        RHS = [scratch(0, 4 * N).rearrange("p (q i) -> p q i", q=4) for _ in range(2)]
        U = [scratch(0, 4 * N).rearrange("p (q i) -> p q i", q=4) for _ in range(2)]
        WU = RHS
        YT = scratch(0, TT)
        YC = scratch(0, TT)
        YQ = scratch(0, TT)
        YR, YS = YT, YQ
        SFIN = scratch(0, 2 * N)
        XX = W[:, 2 * HALF:2 * HALF + C * TT]
        LORA = W[:, W_COLS - BLK:W_COLS]
        QK = [scratch(1, 2 * TT).rearrange("p (n t) -> p n t", n=2) for _ in range(2)]
        VA = [scratch(1, TT).rearrange("p (g i) -> p g i", g=G) for _ in range(2)]
        BIAS = [scratch(1, 6 * P).rearrange("p (h k) -> p h k", h=2) for _ in range(2)]
        SC = scratch(1, 6 * P).rearrange("p (h k) -> p h k", h=2)
        EX = scratch(1, 6 * P).rearrange("p (h k) -> p h k", h=2)
        PN = scratch(1, 6 * P).rearrange("p (h k) -> p h k", h=2)
        PT = scratch(1, 6 * P).rearrange("p (h k) -> p h k", h=2)
        MX = scratch(1, 4).rearrange("p (h s) -> p h s", h=2)
        NMX = scratch(1, 4).rearrange("p (h s) -> p h s", h=2)
        SUM = scratch(1, 4).rearrange("p (h s) -> p h s", h=2)
        RSUM = scratch(1, 4).rearrange("p (h s) -> p h s", h=2)
        areas[2] = [W_COLS, 0]
        SG = scratch(2, 2 * TT).rearrange("p (g f) -> p g f", g=G)
        HM = scratch(2, 2 * TT).rearrange("p (g f) -> p g f", g=G)
        flat = [b.rearrange("p c t -> p (c t)") for b in B]
        ROW = [flat[2][:, 512 * i:512 * i + 512] for i in range(2)]
        SEL = flat[1][:, D:D + TT].rearrange("p (g s) -> p g s", g=G)
        SELW = flat[1][:, D + TT:D + 2 * TT].rearrange("p (g s) -> p g s", g=G)
        SELWT = flat[1][:, D + 2 * TT:D + 3 * TT]
        names = ["LG", "EXL", "PR", "RA", "OH1", "PR2", "OH2", "CH", "WT", "PM"]
        RT = {n: scratch(2, G * NE).rearrange("p (g e) -> p g e", g=G) for n in names}
        R2 = [scratch(2, G) for _ in range(8)]
        CNT = scratch(2, 4 * NE).rearrange("p (n e) -> p n e", n=4)
        JOBP = scratch(2, G * NJ).rearrange("p (g j) -> p g j", g=G)
        JOBW = scratch(2, G * NJ).rearrange("p (g j) -> p g j", g=G)
        JOBE = scratch(2, NJ)
        JT = scratch(2, G * NE).rearrange("p (g e) -> p g e", g=G)
        JOBI = sb("JOBI", NJ + 1, I32)
        HN = B[0].rearrange("p c t -> p (c t)").rearrange("p (g d) -> p g d", g=G)
        YNAT = B[1].rearrange("p c t -> p (c t)").rearrange("p (g d) -> p g d", g=G)
        ACC = B[2]

        col_in, con_in, x_in = sem("col_in"), sem("con_in"), sem("x_in")
        slot_full = [sem(f"slot_full{i}") for i in range(RING)]
        pair_full = [sem(f"pair_full{i}") for i in range(2)]
        apair_full = [sem(f"apair_full{i}") for i in range(2)]
        actx_full = [sem(f"actx_full{i}") for i in range(2)]
        wo_full = [sem(f"wo_full{i}") for i in range(2)]
        lora_full = sem("lora_full")
        wo_psum = [sem(f"wo_psum{i}") for i in range(2)]
        wo_sbuf = [sem(f"wo_sbuf{i}") for i in range(2)]
        eps_ready = sem("eps_ready")
        hi_ready, lo_ready, hi_used, lo_used = sem("hi_ready"), sem("lo_ready"), sem("hi_used"), sem("lo_used")
        cond_hi, cond_split, row_sbuf, mod_psum = (sem("cond_hi"), sem("cond_split"),
                                                             sem("row_sbuf"), sem("mod_psum"))
        xhi_ready, x_split, hm_ready, ht_psum, hhi_ready, hlo_ready = (
            sem("xhi_ready"), sem("x_split"), sem("hm_ready"), sem("ht_psum"), sem("hhi_ready"),
            sem("hlo_ready"))
        yn_sbuf = sem("yn_sbuf")
        cond_ready, mod_ready = sem("cond_ready"), sem("mod_ready")
        sq_ready, sum_ready, root_ready = sem("sq_ready"), sem("sum_ready"), sem("root_ready")
        h_ready, x_ready = sem("h_ready"), sem("x_ready")
        mixed_ready, hid_psum, hid_sbuf = sem("mixed_ready"), sem("hid_psum"), sem("hid_sbuf")
        prep_psum, prep_act, prep_pool, prep_dve = (sem("prep_psum"), sem("prep_act"), sem("prep_pool"),
                                                    sem("prep_dve"))
        chain_psum = [sem(f"chain_psum{i}") for i in range(2)]
        chain_sbuf = [sem(f"chain_sbuf{i}") for i in range(2)]
        gn_psum, gn_sbuf, gn_root, z_ready = sem("gn_psum"), sem("gn_sbuf"), sem("gn_root"), sem("z_ready")
        state_ready, state_out = sem("state_ready"), sem("state_out")
        sg_ready, yt_psum = sem("sg_ready"), sem("yt_psum")
        YT_BANKS = (1, 0, 2, 3)
        qkv_psum, qkv_sbuf, bias_ready = sem("qkv_psum"), sem("qkv_sbuf"), sem("bias_ready")
        kv_out = [sem(f"kv_out{i}") for i in range(2)]
        score_psum, score_ready, exp_ready, prob_ready = (sem("score_psum"), sem("score_ready"),
                                                          sem("exp_ready"), sem("prob_ready"))
        probT_psum, probT_sbuf, att_psum, att_sbuf = (sem("probT_psum"), sem("probT_sbuf"), sem("att_psum"),
                                                      sem("att_sbuf"))
        hn_psum, hn_sbuf, logit_psum, logit_ready, logit_exp = (
            sem("hn_psum"), sem("hn_sbuf"), sem("logit_psum"), sem("logit_ready"), sem("logit_exp"))
        chosen, place_psum, jobs_ready = sem("chosen"), sem("place_psum"), sem("jobs_ready")
        sel_ready, gather_psum = sem("sel_ready"), sem("gather_psum")
        selT_psum, selT_sbuf = sem("selT_psum"), sem("selT_sbuf")
        ey_sbuf, scat_psum, scat_acc = sem("ey_sbuf"), sem("scat_psum"), sem("scat_acc")
        y_out, moe_done = sem("y_out"), sem("moe_done")
        dve_order, last_order, act_order, pool_order = (sem("dve_order"), sem("last_order"), sem("act_order"),
                                                        sem("pool_order"))

        natural_psum = [sem(f"natural_psum{e}") for e in range(2)]
        natural_sbuf = [sem(f"natural_sbuf{e}") for e in range(2)]
        AHEAD = 2
        CH = 17

        loads, had = {}, [0] * RING
        for name, n in (("mod0", MOD_LOADS), ("ffn", FFN_LOADS), ("mod1", MOD_LOADS), ("exp", 0)):
            loads[name] = list(had)
            for m in range(n):
                had[(START[name] + m) % RING] += 1

        def arrived(eng, phase, m, j=0):
            s = (START[phase] + m) % RING
            eng.wait_ge(slot_full[s], 16 * (j * (FFN_LOADS // RING) + loads[phase][s] + m // RING + 1))

        def gu_unit(s, n):
            return n if s == 0 else 4 + 6 * (s - 1) + n

        def down_unit(s, n):
            return 8 + 6 * s + n if s < NS - 1 else 6 * NS - 2 + n

        def wo_tile(l, j, k):
            at = j * D + k * P
            if l == 0 and j >= 6:
                return B[2].rearrange("p c t -> p (c t)")[:, at - 6 * D:at - 6 * D + P]
            at += WO1 if l else 0
            return W[:, at:at + P]

        block = ctx.enter_context(nc.Block())

        @block.sync
        def _(sp):
            def load(phase, m, src):
                s = (START[phase] + m) % RING
                sp.dma_start(W[:, s * LOAD:(s + 1) * LOAD], src).then_inc(slot_full[s], 16)

            def pair_block(c, p):
                src = a["w_rkv"][c] if isinstance(c, int) else \
                    a["w_rkv"][bass.ds(c, 1)].rearrange("a p n -> (a p) n")
                sp.dma_start(W[:, HALF * p:HALF * (p + 1)], src).then_inc(pair_full[p], 16)

            for m in range(MOD_LOADS):
                if m >= RING:
                    sp.wait_ge(lo_ready, 2 * (m - RING + 1))
                load("mod0", m, a["w_mod"][0, m])
            sp.wait_ge(lo_ready, 2 * MOD_LOADS)
            sp.dma_start(LORA, a["w_lora"]).then_inc(lora_full, 16)
            pair_block(0, 0)
            pair_block(1, 1)
            with sp.Fori(0, 3) as i:
                for p in range(2):
                    sp.wait_ge(prep_act, 4 * (2 * i + p) + 2)
                    pair_block(2 * i + p + 2, p)
            sp.wait_ge(prep_psum, 6 * (C - 1) + 3)
            sp.wait_ge(prep_dve, 6 * (C - 1) + 1)
            sp.dma_start(W[:, 0:6 * D], a["w_o"][0, :, 0:6 * D]).then_inc(wo_full[0], 16)
            sp.dma_start(B[2].rearrange("p c t -> p (c t)"), a["w_o"][0, :, 6 * D:8 * D]).then_inc(wo_full[1], 16)
            sp.wait_ge(state_ready, C)
            sp.wait_ge(state_out, 16 * C)
            sp.wait_ge(z_ready, C)
            for m in range(FFN_LOADS):
                if (START["ffn"] + m) % RING == 0 and m < RING:
                    sp.wait_ge(wo_psum[0], 4)
                if m >= RING:
                    sp.wait_ge(lo_ready, UNITS["ffn"] + 2 * (m - RING + 1))
                load("ffn", m, a["w_ffn"][m])
            for m in range(MOD_LOADS):
                sp.wait_ge(lo_ready, UNITS["mod1"] + 2 * (m - RING + 1))
                load("mod1", m, a["w_mod"][1, m])
            sp.wait_ge(lo_ready, UNITS["exp"])

            def attention_block(c, p, cols, full):
                src = a["w_qkv"][c][:, cols] if isinstance(c, int) else \
                    a["w_qkv"][bass.ds(c, 1), :, cols].rearrange("a p n -> (a p) n")
                sp.dma_start(W[:, HALF * p + cols.start:HALF * p + cols.stop], src).then_inc(full[p], 16)

            weights, context = slice(0, BLK), slice(BLK, HALF)
            for c in range(2):
                attention_block(c, c, weights, apair_full)
                attention_block(c, c, context, actx_full)
            sp.dma_start(W[:, WO1:W_COLS], a["w_o"][1]).then_inc(wo_full[1], 16)
            with sp.Fori(0, 3) as i:
                for p in range(2):
                    sp.wait_ge(qkv_psum, 2 * (2 * i + p) + 2)
                    attention_block(2 * i + p + 2, p, weights, apair_full)
                    sp.wait_ge(att_psum, 2 * i + p + 1)
                    attention_block(2 * i + p + 2, p, context, actx_full)
            sp.wait_ge(att_sbuf, C)
            sp.wait_ge(kv_out[0], 32 * C // 2)
            sp.wait_ge(kv_out[1], 32 * C // 2)

            def job(j, e, following, first=1):
                for m in range(first, FFN_LOADS + 1):
                    sp.wait_ge(lo_ready, 2 * FFN_LOADS * j + UNITS["exp"] + 2 * (m - RING + 1))
                    e, n = (e, m) if m < FFN_LOADS else (following, 0)
                    src = a["w_exp"][e, n] if isinstance(e, int) else \
                        a["w_exp"][bass.ds(e, 1), n].rearrange("a p n -> (a p) n")
                    load("exp", m, src)

            for m in range(RING):
                if (START["exp"] + m) % RING == WO1 // LOAD:
                    sp.wait_ge(wo_psum[1], 4)
                load("exp", m, a["w_exp"][0, m])
            job(0, 0, 1, RING)
            with sp.Fori(1, NE - 1) as j:
                job(j, j, j + 1)
            sp.wait_ge(jobs_ready, 1)

            def listed(j):
                return sp.value_load(JOBI[0:1, j], min_val=0, max_val=NE - 1)

            job(NE - 1, NE - 1, listed(slice(NE, NE + 1)))
            over = sp.value_load(JOBI[0:1, NJ:NJ + 1], min_val=0, max_val=NOVER)
            with sp.Fori(0, over) as j:
                job(j + NE, listed(bass.ds(j + NE, 1)), listed(bass.ds(j + NE + 1, 1)))
            for b in range(4):
                sp.wait_ge(x_ready, 4 * 3 + b + 1)
                sp.dma_start(a["out_x"][:, 2 * b:2 * b + 2], XT[:, 2 * b:2 * b + 2]).then_inc(y_out, 16)
            sp.wait_ge(y_out, 4 * 16)

        @block.tensor
        def _(pe):
            mm = nc.tensor.matmul

            def unit(phase, u, j, by_hi, by_lo):
                at = 2 * FFN_LOADS * j + UNITS[phase] + u
                pe.wait_ge(hi_ready, at + 1)
                by_hi(HI[:, u % NBUF]).then_inc(hi_used, 1)
                pe.wait_ge(lo_ready, at + 1)
                by_lo(LO[:, u % NBUF]).then_inc(lo_used, 1)

            def modulation(l):
                phase = f"mod{l}"
                pe.wait_ge(cond_split, l + 1)

                def turn(t):
                    pe.wait_ge(row_sbuf, MOD_TILES * l + t + 1)
                    for f in range(4):
                        j = 4 * t + f
                        last = mm(PS[2][:, 2 * j:2 * j + 2], ROW[t % 2][0:4, P * f:P * f + P], con("join")[0:4],
                                  start=True, stop=True)
                    last.then_inc(mod_psum, 1)

                if l == 0:
                    pe.wait_ge(con_in, 16)
                for t in range(MOD_TILES):
                    if MOD_TILES * l + t >= 2:
                        pe.wait_ge(row_sbuf, MOD_TILES * l + t - 1)

                    for n in range(4):
                        def part(w, first, end):
                            for k in range(2):
                                last = mm(PS[t % 2], XHI[:, 2 * n + k, 0:P], w[:, 512 * k:512 * k + 512],
                                          start=first and k == 0, stop=end and k == 1)
                            return last
                        unit(phase, 4 * t + n, 0, lambda w: part(w, n == 0, False), lambda w: part(w, False, n == 3))
                    if t:
                        turn(t - 1)
                turn(MOD_TILES - 1)

            def norm_part(n, i, b, squares):
                pe.wait_ge(sq_ready, 4 * (n - 1) + i + 1)
                for k in range(2):
                    last = mm(PS[1][:, 0:TT], ONES, squares[:, 2 * b + k], start=(i == 0 and k == 0),
                              stop=(i == 3 and k == 1))
                if i == 3:
                    last.then_inc(sum_ready, 1)

            def norm_sum(n, chunks=range(4)):
                for i, b in enumerate(chunks):
                    norm_part(n, i, b, B[1])

            def project_out(l, src):
                squares = B[1 + l]
                pe.wait_ge(wo_full[l], 16 * (l + 1))
                if l == 0:
                    pe.wait_ge(wo_full[1], 16)
                for b in range(4):
                    if b >= 2:
                        pe.wait_ge(wo_sbuf[l], b - 1)
                    for half in range(2):
                        for kc in range(C):
                            last = mm(PS[2 + b % 2][:, TT * half:TT * half + TT], wo_tile(l, 2 * b + half, kc),
                                      src[:, kc], start=(kc == 0), stop=(kc == C - 1))
                    last.then_inc(wo_psum[l], 1)
                    if b:
                        norm_part(2 + 4 * l, b - 1, b - 1, squares)
                norm_part(2 + 4 * l, 3, 3, squares)

            def wblock(p):
                blk = W[:, HALF * p:HALF * (p + 1)]
                return (blk[:, 0:BLK].rearrange("p (n k m) -> p n k m", n=3, k=C),
                        blk[:, BLK:BLK + 384].rearrange("p (n m) -> p n m", n=3))

            def prep_rkv(c, r, p):
                w, w2 = wblock(p)
                pe.wait_ge(pair_full[p], 16 * (r + 1))
                if not (isinstance(c, int) and c == 0):
                    pe.wait_ge(prep_act, 4 * (c - 1) + 2)
                for n in range(2):
                    for kc in range(C):
                        last = mm(PS[4][:, TT * n:TT * n + TT], w[:, n, kc], B[n][:, kc],
                                  start=(kc == 0), stop=(kc == C - 1))
                last.then_inc(prep_psum, 1)
                for kc in range(C):
                    mm(PS[5][:, 0:TT], w[:, 2, kc], B[2][:, kc], start=(kc == 0), stop=(kc == C - 1))
                mm(PS[5][:, TT:2 * TT], w2[:, 2], HID[:, 2], start=True, stop=True).then_inc(prep_psum, 1)

            def prep_lora(c, p):
                _, w2 = wblock(p)
                pe.wait_ge(prep_act, 4 * c + 1)
                for n in range(2):
                    for e in range(2):
                        rows = slice(N * e, N * e + N)
                        last = mm(PS[4 + e][:, TT * n:TT * n + TT], w2[rows, n], HID[rows, n],
                                  start=True, stop=True)
                last.then_inc(prep_psum, 1)

            def prep_norm(c):
                pe.wait_ge(prep_pool, 3 * c + 1)
                if not (isinstance(c, int) and c == 0):
                    pe.wait_ge(prep_dve, 6 * (c - 1) + 6)
                mm(PS[6][:, 0:TT], HEADS, SQ, start=True, stop=True).then_inc(prep_psum, 1)

            def prep_coef(c):
                pe.wait_ge(prep_pool, 3 * c + 3)
                pe.wait_ge(prep_dve, 6 * c + 2)
                mm(PS[6][:, 0:TT], HEADS, COEF, start=True, stop=True)
                for g in range(G):
                    last = nc.tensor.transpose(PS[6][:, TT + P * g:TT + P * g + P], RKV[:, 2, P * g:P * g + P],
                                               IDENT)
                last.then_inc(prep_psum, 1)

            def prep_hat(c):
                pe.wait_ge(prep_dve, 6 * c + 5)
                for n in range(4):
                    last = nc.tensor.transpose(PS[6][:, P * n:P * n + P], HATT[:, n], IDENT)
                last.then_inc(prep_psum, 1)

            def heads(q):
                hl, g = q // 2, q % 2
                return slice(N * hl, N * hl + N), slice(T * g, T * g + T)

            def gram(e, c, p, k):
                if k > 1 or not (isinstance(c, int) and c == 0):
                    pe.wait_ge(chain_sbuf[e], CH * c + k - 1)
                if k == 1:
                    pe.wait_ge(prep_pool, 3 * c + 3)
                for q in range(4):
                    rows, cs = heads(q)
                    bank = PS[2 * e + q // 2]
                    if k < 3:
                        lhs = (BT if k == 1 else KT)[p][rows, e, cs]
                        rhs = AR[p][e][rows, :, cs]
                        out = bank[:, 256 * (q % 2):256 * (q % 2) + 256].rearrange("p (k t) -> p k t", k=2)
                    else:
                        lhs, rhs = AR[p][e][rows, 0, cs], BT[p][rows, e, cs]
                        out = bank[:, P * (q % 2):P * (q % 2) + P]
                    last = mm(out, lhs, rhs, start=True, stop=True)
                last.then_inc(chain_psum[e], 1)

            def level_z(e, c, n):
                pe.wait_ge(natural_sbuf[e], 5 * c + n)
                for q in range(4):
                    last = mm(PS[2 * e][:, P * q:P * q + P], GB[e][:, q, 0], TN[e][:, q], start=True, stop=True)
                last.then_inc(chain_psum[e], 1)

            def level_d(e, c, n):
                pe.wait_ge(chain_sbuf[e], CH * c + 2 * n + 2)
                if n < 5:
                    for q in range(4):
                        last = mm(PS[2 * e][:, P * q:P * q + P], TR[e][:, q], Z[e][:, q], start=True, stop=True)
                    last.then_inc(natural_psum[e], 1)
                for q in range(4):
                    last = mm(PS[2 * e + 1][:, P * q:P * q + P], Z[e][:, q], TR[e][:, q], start=True, stop=True)
                last.then_inc(chain_psum[e], 1)

            def right_side(e, c, p):
                pe.wait_ge(chain_sbuf[e], CH * c + 13)
                pe.wait_ge(prep_dve, 6 * c + 5)
                for q in range(4):
                    rows, cs = heads(q)
                    out = PS[2 * e + q // 2][:, N * (q % 2):N * (q % 2) + N]
                    mm_last = mm(out, GK[e][:, q, 0], VN[p][:, q % 2, rows], start=True, stop=(q % 2 == 0))
                    if q % 2:
                        mm_last = mm(out, AR[p][e][rows, 0, cs], S0P[p][rows, e], start=False, stop=True)
                mm_last.then_inc(chain_psum[e], 1)

            def solve0(e, c):
                pe.wait_ge(chain_sbuf[e], CH * c + 14)
                for q in range(4):
                    last = mm(PS[2 * e][:, N * q:N * q + N], TR[e][:, q], RHS[e][:, q], start=True, stop=True)
                last.then_inc(chain_psum[e], 1)

            def halves(e):
                return (slice(0, 64), slice(64, 128)) if e == 0 else (slice(64, 128), slice(0, 64))

            def solve1(e, c):
                first, _ = halves(e)
                pe.wait_ge(chain_sbuf[e], CH * c + 15)
                for q in range(4):
                    last = mm(PS[2 * e + 1][:, N * q:N * q + N], GB[e][first, q, 0], U[e][first, q],
                              start=True, stop=True)
                last.then_inc(chain_psum[e], 1)

            def solve2(e, c):
                _, then = halves(e)
                pe.wait_ge(chain_sbuf[e], CH * c + 16)
                for q in range(4):
                    last = mm(PS[2 * e][:, N * q:N * q + N], TR[e][then, q], WU[e][then, q],
                              start=True, stop=True)
                last.then_inc(chain_psum[e], 1)

            def outputs(c, p):
                for e in range(2):
                    pe.wait_ge(chain_sbuf[e], CH * c + 17)
                pe.wait_ge(prep_dve, 6 * c + 6)
                if not (isinstance(c, int) and c == 0):
                    pe.wait_ge(gn_root, c)
                for q in range(4):
                    rows, cs = heads(q)
                    out = PS[7][rows, cs]
                    mm(out, VN[p][:, q % 2, rows], GK[0][:, q, 1], start=True, stop=False)
                    mm(out, VN[p][:, q % 2, rows], GK[1][:, q, 1], start=False, stop=False)
                    if q % 2:
                        mm(out, S0P[p][rows, 0], AR[p][0][rows, 1, cs], start=False, stop=False)
                        mm(out, S0P[p][rows, 1], AR[p][1][rows, 1, cs], start=False, stop=False)
                    mm(out, U[0][:, q], GB[0][:, q, 1], start=False, stop=False)
                    mm(out, U[1][:, q], GB[1][:, q, 1], start=False, stop=True)
                for hl in range(2):
                    for e in range(2):
                        rows = slice(N * hl, N * hl + N)
                        out = PS[7][rows, TT + N * e:TT + N * e + N]
                        mm(out, U[e][:, 2 * hl], HATN[p][:, 2 * e, rows], start=True, stop=False)
                        last = mm(out, VN[p][:, 0, rows], HATN[p][:, 2 * e + 1, rows], start=False, stop=True)
                last.then_inc(gn_psum, 1)

            def gn_mean(c):
                pe.wait_ge(gn_sbuf, 2 * c + 1)
                mm(PS[7][:, 0:TT], HEADS, YT, start=True, stop=True).then_inc(gn_psum, 1)

            def gn_var(c):
                pe.wait_ge(gn_sbuf, 2 * c + 2)
                mm(PS[7][:, 0:TT], HEADS, YQ, start=True, stop=True).then_inc(gn_psum, 1)

            def mix_step(c, p, prep, tail):
                for e in range(2):
                    gram(e, c, p, 1)
                if tail:
                    gn_mean(c - 1)
                if prep is not None:
                    prep_rkv(*prep)
                if tail:
                    gn_var(c - 1)
                for e in range(2):
                    gram(e, c, p, 2)
                if prep is not None:
                    prep_lora(prep[0], prep[2])
                for e in range(2):
                    gram(e, c, p, 3)
                if prep is not None:
                    prep_norm(prep[0])
                for n in range(1, 6):
                    for e in range(2):
                        level_z(e, c, n)
                    for e in range(2):
                        level_d(e, c, n)
                    if prep is not None and n == 4:
                        prep_coef(prep[0])
                if prep is not None:
                    prep_hat(prep[0])
                for e in range(2):
                    right_side(e, c, p)
                for f in (solve0, solve1, solve2):
                    for e in range(2):
                        f(e, c)
                outputs(c, p)

            modulation(0)
            norm_sum(1)
            pe.wait_ge(lora_full, 16)
            w1 = LORA.rearrange("p (n k m) -> p n k m", n=3, k=C)
            for n in range(3):
                pe.wait_ge(mixed_ready, n + 1)
                for kc in range(C):
                    last = mm(PS[2 + n][:, 0:TT], w1[:, n, kc], B[n][:, kc], start=(kc == 0), stop=(kc == C - 1))
                last.then_inc(hid_psum, 1)
            pe.wait_ge(hid_sbuf, 3)
            pe.wait_ge(mixed_ready, 6)
            prep_rkv(0, 0, 0)
            prep_lora(0, 0)
            prep_norm(0)
            prep_coef(0)
            prep_hat(0)
            mix_step(0, 0, (1, 0, 1), False)
            with pe.Fori(0, 3) as i:
                mix_step(2 * i + 1, 1, (2 * i + 2, i + 1, 0), True)
                mix_step(2 * i + 2, 0, (2 * i + 3, i + 1, 1), True)
            mix_step(7, 1, None, True)
            gn_mean(7)
            gn_var(7)
            pe.wait_ge(z_ready, C)
            project_out(0, HT)
            norm_sum(3)

            def gate_up(phase, base, j, s, n, groups):
                def by(parts):
                    def run(w):
                        for g in range(groups):
                            for k in range(2):
                                for i, x in enumerate(parts):
                                    last = mm(PS[2 * (s % 2) + g], x[:, 2 * n + k, T * g:T * g + T],
                                              w[:, 512 * k:512 * k + 512],
                                              start=(n == 0 and k == 0 and i == 0 and len(parts) == 2),
                                              stop=(n == 3 and k == 1 and len(parts) == 1))
                        return last
                    return run
                unit(phase, gu_unit(s, n), j, by((XHI, XLO)), by((XHI,)))

            def turn_hidden(base, s, groups):
                pe.wait_ge(hm_ready, base + s + 1)
                for g in range(groups):
                    for f in range(2):
                        at = T * (groups * f + g)
                        last = nc.tensor.transpose(PS[2 * (s % 2)][:, at:at + T], HM[:, g, P * f:P * f + P], IDENT)
                last.then_inc(ht_psum, 1)

            def down(phase, base, j, s, groups):
                pe.wait_ge(hhi_ready, base + s + 1)
                pe.wait_ge(hlo_ready, base + s + 1)
                for f in range(2):
                    def by(parts):
                        def run(w):
                            for g in range(groups):
                                for half in range(2):
                                    for i, h in enumerate(parts):
                                        last = mm(PS[4 + 2 * g + half], h[:, f, T * g:T * g + T],
                                                  w[:, 512 * half:512 * half + 512],
                                                  start=(s == 0 and f == 0 and i == 0 and len(parts) == 2),
                                                  stop=(s == NS - 1 and f == 1 and len(parts) == 1))
                            return last
                        return run
                    unit(phase, down_unit(s, f), j, by((HHI, HLO)), by((HHI,)))

            def swiglu(phase, base, j, groups, between):
                for s in range(NS):
                    if phase == "exp" and s == 1:
                        pe.wait_ge(selT_sbuf, j + 1)
                    for n in range(4):
                        gate_up(phase, base, j, s, n, groups)
                        if n == 1 and s:
                            turn_hidden(base, s - 1, groups)
                    if s:
                        down(phase, base, j, s - 1, groups)
                turn_hidden(base, NS - 1, groups)
                between()
                down(phase, base, j, NS - 1, groups)

            pe.wait_ge(x_split, 1)
            swiglu("ffn", 0, 0, G, lambda: None)
            pe.wait_ge(yn_sbuf, 1)
            for c in range(C):
                for g in range(G):
                    last = nc.tensor.transpose(PS[c // 2][:, TT * (c % 2) + T * g:TT * (c % 2) + T * g + T],
                                               YNAT[:, g, P * c:P * c + P], IDENT)
            last.then_inc(yt_psum, 1)
            norm_sum(4, YT_BANKS)
            modulation(1)
            norm_sum(5)

            def qkv(c, r, p):
                w = W[:, HALF * p:HALF * p + BLK].rearrange("p (n k m) -> p n k m", n=3, k=C)
                pe.wait_ge(apair_full[p], 16 * (r + 1))
                if not (isinstance(c, int) and c == 0):
                    pe.wait_ge(qkv_sbuf, 2 * c)
                for n in range(2):
                    for kc in range(C):
                        last = mm(PS[0][:, TT * n:TT * n + TT], w[:, n, kc], HT[:, kc],
                                  start=(kc == 0), stop=(kc == C - 1))
                last.then_inc(qkv_psum, 1)
                for g in range(G):
                    for kc in range(C):
                        last = mm(PS[1][:, P * g:P * g + P], HT[:, kc, T * g:T * g + T], w[:, 2, kc],
                                  start=(kc == 0), stop=(kc == C - 1))
                last.then_inc(qkv_psum, 1)

            def scores(c, p):
                ctx_k = W[:, HALF * p + BLK + 2 * P:HALF * p + BLK + 3 * P]
                pe.wait_ge(actx_full[p], 8 * (c - p) + 16)
                pe.wait_ge(qkv_sbuf, 2 * c + 2)
                if not (isinstance(c, int) and c == 0):
                    pe.wait_ge(score_ready, 2 * c - 1)
                for hl in range(2):
                    rows = slice(N * hl, N * hl + N)
                    for g in range(G):
                        mm(PS[2 + hl][:, P * g:P * g + P], QK[p][rows, 0, T * g:T * g + T],
                           QK[p][rows, 1, T * g:T * g + T], start=True, stop=True)
                    last = mm(PS[2 + hl][:, 2 * P:3 * P], QK[p][rows, 0, T:2 * T], ctx_k[rows],
                              start=True, stop=True)
                last.then_inc(score_psum, 1)

            def attend(c, p, r):
                ctx_v = W[:, HALF * p + BLK + 3 * P:HALF * (p + 1)]
                if r is not None:
                    qkv(c + 1, r, 1 - p)
                pe.wait_ge(prob_ready, c + 1)
                if not (isinstance(c, int) and c == 0):
                    pe.wait_ge(probT_sbuf, c)
                for hl in range(2):
                    for n in range(3):
                        last = nc.tensor.transpose(PS[4 + hl][:, P * n:P * n + P], PN[:, hl, P * n:P * n + P], IDENT)
                last.then_inc(probT_psum, 1)
                if r is not None:
                    scores(c + 1, 1 - p)
                pe.wait_ge(probT_sbuf, c + 1)
                if not (isinstance(c, int) and c == 0):
                    pe.wait_ge(att_sbuf, c)
                for hl in range(2):
                    rows = slice(N * hl, N * hl + N)
                    mm(PS[6][rows, 0:T], VA[p][:, 0, rows], PT[:, hl, 0:P], start=True, stop=True)
                    mm(PS[6][rows, T:2 * T], VA[p][:, 1, rows], PT[:, hl, P:2 * P], start=True, stop=False)
                    last = mm(PS[6][rows, T:2 * T], ctx_v[:, rows], PT[:, hl, 2 * P:3 * P], start=False, stop=True)
                last.then_inc(att_psum, 1)

            pe.wait_ge(h_ready, 3)
            qkv(0, 0, 0)
            scores(0, 0)
            attend(0, 0, 0)
            with pe.Fori(0, 3) as i:
                attend(2 * i + 1, 1, i + 1)
                attend(2 * i + 2, 0, i + 1)
            attend(7, 1, None)
            pe.wait_ge(att_sbuf, C)
            project_out(1, B[1])
            norm_sum(7)

            pe.wait_ge(h_ready, 4)
            for g in range(G):
                for c in range(C):
                    last = nc.tensor.transpose(PS[2 * g + c // 4][:, P * (c % 4):P * (c % 4) + P],
                                               HT[:, c, T * g:T * g + T], IDENT)
            last.then_inc(hn_psum, 1)
            rw = col("router_w").rearrange("p (c e) -> p c e", c=C)
            for g in range(G):
                for c in range(C):
                    last = mm(PS[4][:, NE * g:NE * g + NE], HT[:, c, T * g:T * g + T], rw[:, c],
                              start=(c == 0), stop=(c == C - 1))
            last.then_inc(logit_psum, 1)
            pe.wait_ge(chosen, 1)
            ch = RT["CH"]
            mm(PS[5][:, 0:NE], SEEN[:, 0, 0], ch[:, 0], start=True, stop=True)
            mm(PS[5][:, NE:2 * NE], ONES, ch[:, 0], start=True, stop=False)
            mm(PS[5][:, NE:2 * NE], SEEN[:, 0, 0], ch[:, 1], start=False, stop=True)
            mm(PS[5][:, 2 * NE:3 * NE], ONES, ch[:, 0], start=True, stop=False)
            mm(PS[5][:, 2 * NE:3 * NE], ONES, ch[:, 1], start=False, stop=True).then_inc(place_psum, 1)
            pe.wait_ge(hn_sbuf, 1)

            def gather(j):
                pe.wait_ge(sel_ready, j + 1)
                if not (isinstance(j, int) and j == 0):
                    pe.wait_ge(scat_acc, 4 * (j - 1) + 1)
                for c in range(C):
                    for g in range(G):
                        last = mm(PS[1 + 2 * (c // 4)][:, P * (c % 4):P * (c % 4) + P], HN[:, g, P * c:P * c + P],
                                  SEL[:, g], start=(g == 0), stop=(g == G - 1))
                last.then_inc(gather_psum, 1)

            def turn_weights(j):
                pe.wait_ge(sel_ready, j + 1)
                for g in range(G):
                    last = nc.tensor.transpose(PS[2][:, P * g:P * g + P], SELW[:, g], IDENT)
                last.then_inc(selT_psum, 1)

            def job(j):
                pe.wait_ge(x_split, j + 2)
                swiglu("exp", NS * j + NS, j, 1, lambda: gather(j + 1))
                turn_weights(j + 1)
                pe.wait_ge(ey_sbuf, j + 1)
                for b in range(4):
                    if b == 2:
                        pe.wait_ge(x_split, j + 3)
                    for half in range(2):
                        c = 2 * b + half
                        last = mm(PS[(6, 7, 1, 3)[b]][:, TT * half:TT * half + TT], YNAT[:, 0, P * c:P * c + P],
                                  SELWT, start=True, stop=True)
                    last.then_inc(scat_psum, 1)

            gather(0)
            turn_weights(0)
            with pe.Fori(0, NE) as j:
                job(j)
            over = pe.value_load(JOBI[0:1, NJ:NJ + 1], min_val=0, max_val=NOVER)
            with pe.Fori(0, over) as j:
                job(j + NE)
            norm_sum(8)

        @block.scalar
        def _(act):
            order = Order(act, act_order)
            fn = nc.scalar.activation
            act.dma_start(COL, a["cols"]).then_inc(col_in, 16)
            act.dma_start(XT, a["x"]).then_inc(x_in, 16)
            act.dma_start(CON, a["cons"]).then_inc(con_in, 16)
            act.wait_ge(col_in, 16)
            fn(COND, col("cond").rearrange("p (c g) -> p c g", g=G), ACT.Silu).then_inc(cond_ready, 1)

            def split(phase, u, j=0):
                at = 2 * FFN_LOADS * j + UNITS[phase] + u
                if u % 2 == 0:
                    arrived(act, phase, u // 2, j)
                if not isinstance(at, int) or at >= NBUF:
                    act.wait_ge(hi_used, at - NBUF + 1)
                    act.wait_ge(lo_ready, at - NBUF + 1)
                fn(HI[:, u % NBUF], raw_unit(phase, u), ACT.Copy).then_inc(hi_ready, 1)

            def condition(l):
                act.wait_ge(cond_hi, 2 * l + 1)
                if l == 0:
                    act.wait_ge(cond_ready, 1)
                fn(XHI[:, :, 0:G], COND, ACT.Copy).then_inc(cond_hi, 1)

            def modulation(l):
                def row(t):
                    act.wait_ge(lo_used, UNITS[f"mod{l}"] + 4 * t + 4)
                    if MOD_TILES * l + t >= 2:
                        act.wait_ge(mod_psum, MOD_TILES * l + t - 1)
                    fn(ROW[t % 2][0:4], PS[t % 2][0:4], ACT.Copy).then_inc(row_sbuf, 1)

                for t in range(MOD_TILES):
                    for n in range(4):
                        split(f"mod{l}", 4 * t + n)
                        if n == 2 and t:
                            row(t - 1)
                row(MOD_TILES - 1)

            def square(b, src, dst=B[1]):
                fn(dst[:, 2 * b:2 * b + 2], src, ACT.Square).then_inc(sq_ready, 1)

            def norm_root(n):
                act.wait_ge(sum_ready, n)
                if n >= 2:
                    act.wait_ge(x_ready if n % 2 else h_ready, 4 * (n // 2) if n % 2 else n // 2)
                fn(RMS, PS[1][:, 0:TT], ACT.Sqrt, scale=1.0 / D, bias=BIASES[:, 0:1]).then_inc(root_ready, 1)

            def norm(n, src):
                for b in range(4):
                    if src is XT and n > 1:
                        act.wait_ge(x_ready, 4 * (n // 2 - 1) + b + 1)
                    square(b, src[:, 2 * b:2 * b + 2])
                norm_root(n)

            def wo_out(l):
                for b in range(4):
                    act.wait_ge(wo_psum[l], b + 1)
                    bank = PS[2 + b % 2].rearrange("p (c t) -> p c t", c=2)
                    square(b, bank, B[1 + l])
                    fn(B[0][:, 2 * b:2 * b + 2], bank, ACT.Copy).then_inc(wo_sbuf[l], 1)
                norm_root(2 + 4 * l)

            condition(0)
            modulation(0)
            act.wait_ge(x_in, 16)
            act.wait_ge(eps_ready, 1)
            norm(1, XT)
            act.wait_ge(hid_psum, 1)
            fn(HID[:, 0], PS[2][:, 0:TT], ACT.Tanh).then_inc(hid_sbuf, 1)
            act.wait_ge(hid_psum, 2)
            fn(HID[:, 1], PS[3][:, 0:TT], ACT.Copy).then_inc(hid_sbuf, 1)
            act.wait_ge(hid_psum, 3)
            fn(HID[:, 2], PS[4][:, 0:TT], ACT.Sigmoid).then_inc(hid_sbuf, 1)

            def prep_rkv(c, p):
                first = isinstance(c, int) and c == 0
                act.wait_ge(prep_psum, 6 * c + 1)
                if not first:
                    act.wait_ge(prep_pool, 3 * c)
                fn(RKV[:, 0:2], PS[4].rearrange("p (n t) -> p n t", n=2), ACT.Copy)
                act.wait_ge(prep_psum, 6 * c + 2)
                if not first:
                    act.wait_ge(prep_dve, 6 * c)
                    act.wait_ge(z_ready, c - 1)
                fn(RKV[:, 2], PS[5][:, 0:TT], ACT.Copy)
                fn(GATE[p], PS[5][:, TT:2 * TT], ACT.Copy).then_inc(prep_act, 1)

            def prep_tanh(c, p):
                act.wait_ge(prep_psum, 6 * c + 3)
                act.wait_ge(prep_dve, 6 * c + 1)
                for e in range(2):
                    fn(THW[:, e], PS[4 + e][:, 0:TT], ACT.Tanh, scale=0.5, bias=PP[p][:, e:e + 1])
                for e in range(2):
                    last = fn(THA[:, e], PS[4 + e][:, TT:2 * TT], ACT.Tanh, scale=0.5,
                              bias=PP[p][:, 2 + e:3 + e])
                order(last)
                order(fn(LD, THW, ACT.Identity, scale=-0.5 * DECAY, bias=BIASES[:, 2:3]))
                order(fn(THW, THA, ACT.Identity, scale=PP[p][:, 5:6], bias=PP[p][:, 6:7]))
                fn(THA, THA, ACT.Identity, scale=-0.5, bias=BIASES[:, 3:4]).then_inc(prep_act, 1)

            def prep_root(c):
                act.wait_ge(prep_dve, 6 * c + 2)
                fn(ROOT, SQ, ACT.Sqrt).then_inc(prep_act, 1)

            def prep_exp(c):
                act.wait_ge(prep_dve, 6 * c + 3)
                fn(PW, CUM, ACT.Exp)
                act.wait_ge(prep_pool, 3 * c + 2)
                fn(PINV, CUM, ACT.Exp, scale=-1.0)
                fn(PX, CUX, ACT.Exp).then_inc(prep_act, 1)

            def right_side(e, c):
                act.wait_ge(chain_psum[e], CH * c + 14)
                for hl in range(2):
                    last = fn(RHS[e][:, 2 * hl:2 * hl + 2],
                              PS[2 * e + hl][:, 0:2 * N].rearrange("p (q i) -> p q i", q=2), ACT.Copy)
                last.then_inc(chain_sbuf[e], 1)

            def solve0(e, c):
                act.wait_ge(chain_psum[e], CH * c + 15)
                fn(U[e], PS[2 * e][:, 0:4 * N].rearrange("p (q i) -> p q i", q=4), ACT.Copy)\
                    .then_inc(chain_sbuf[e], 1)

            def solve1(e, c):
                then = slice(64, 128) if e == 0 else slice(0, 64)
                act.wait_ge(chain_psum[e], CH * c + 16)
                fn(WU[e][then], PS[2 * e + 1][then, 0:4 * N].rearrange("p (q i) -> p q i", q=4), ACT.Copy)\
                    .then_inc(chain_sbuf[e], 1)

            def outputs(c):
                act.wait_ge(gn_psum, 3 * c + 1)
                if not (isinstance(c, int) and c == 0):
                    act.wait_ge(state_out, 16 * c)
                fn(SFIN, PS[7][:, TT:TT + 2 * N], ACT.Copy).then_inc(state_ready, 1)
                fn(YT, PS[7][:, 0:TT], ACT.Copy).then_inc(gn_sbuf, 1)
                act.wait_ge(state_ready, c + 1)
                dst = a["out_state"][c] if isinstance(c, int) else \
                    a["out_state"][bass.ds(c, 1)].rearrange("a p n -> (a p) n")
                act.dma_start(dst, SFIN).then_inc(state_out, 16)

            def gn_root_(c):
                act.wait_ge(gn_psum, 3 * c + 3)
                fn(YR, PS[7][:, 0:TT], ACT.Sqrt, scale=1.0 / N, bias=BIASES[:, 1:2]).then_inc(gn_root, 1)

            def mix_step(c, prep, tail):
                if tail:
                    gn_root_(c - 1)
                if prep is not None:
                    prep_rkv(*prep)
                    prep_tanh(*prep)
                    prep_root(prep[0])
                    prep_exp(prep[0])
                for f in (right_side, solve0, solve1):
                    for e in range(2):
                        f(e, c)
                outputs(c)

            prep_rkv(0, 0)
            prep_tanh(0, 0)
            prep_root(0)
            prep_exp(0)
            mix_step(0, (1, 1), False)
            with act.Fori(0, 3) as i:
                order.enter(i, STEPS_ACT_MIX)
                mix_step(2 * i + 1, (2 * i + 2, 0), True)
                mix_step(2 * i + 2, (2 * i + 3, 1), True)
                order.leave(3)
            mix_step(7, None, True)
            gn_root_(7)
            wo_out(0)
            norm(3, XT)

            def swiglu(phase, base, j, groups):
                width = T * groups

                def gate(s):
                    act.wait_ge(lo_used, 2 * FFN_LOADS * j + UNITS[phase] + gu_unit(s, 3) + 1)
                    if not (phase == "ffn" and s == 0):
                        act.wait_ge(hm_ready, base + s)
                    for g in range(groups):
                        last = fn(SG[:, g], PS[2 * (s % 2) + g][:, 0:FB], ACT.Silu)
                    last.then_inc(sg_ready, 1)

                def hidden(s):
                    act.wait_ge(ht_psum, base + s + 1)
                    if s:
                        act.wait_ge(lo_used, 2 * FFN_LOADS * j + UNITS[phase] + down_unit(s - 1, 1) + 1)
                    fn(HHI[:, :, 0:width], PS[2 * (s % 2)][:, 0:2 * width].rearrange("p (f t) -> p f t", f=2),
                       ACT.Copy).then_inc(hhi_ready, 1)

                for s in range(NS):
                    for n in range(4):
                        if phase == "ffn" or gu_unit(s, n) >= AHEAD:
                            split(phase, gu_unit(s, n), j)
                        if n == 0 and s:
                            gate(s - 1)
                    if s:
                        hidden(s - 1)
                        for f in range(2):
                            split(phase, down_unit(s - 1, f), j)
                gate(NS - 1)
                for f in range(2):
                    split(phase, down_unit(NS - 1, f), j)

                return hidden

            act.wait_ge(h_ready, 2)
            fn(XHI, HT, ACT.Copy).then_inc(xhi_ready, 1)
            swiglu("ffn", 0, 0, G)(NS - 1)
            act.wait_ge(lo_used, UNITS["mod1"])
            for g in range(G):
                for half in range(2):
                    last = fn(YNAT[:, g, 512 * half:512 * half + 512], PS[4 + 2 * g + half], ACT.Copy)
            last.then_inc(yn_sbuf, 1)
            act.wait_ge(yt_psum, 1)
            for b in YT_BANKS:
                bank = PS[b].rearrange("p (c t) -> p c t", c=2)
                fn(B[0][:, 2 * b:2 * b + 2], bank, ACT.Copy)
                square(b, bank)
            norm_root(4)
            condition(1)
            modulation(1)
            norm(5, XT)

            def attend_in(c, p):
                act.wait_ge(qkv_psum, 2 * c + 1)
                if not isinstance(c, int) or c >= 2:
                    half = (c - p) * 8
                    act.wait_ge(kv_out[p], 2 * half)
                    act.wait_ge(att_psum, c - 1)
                fn(QK[p], PS[0].rearrange("p (n t) -> p n t", n=2), ACT.Copy).then_inc(qkv_sbuf, 1)
                act.wait_ge(qkv_psum, 2 * c + 2)
                fn(VA[p], PS[1][:, 0:TT].rearrange("p (g i) -> p g i", g=G), ACT.Copy).then_inc(qkv_sbuf, 1)

            def attend(c, nxt):
                act.wait_ge(score_ready, 2 * c + 2)
                if not (isinstance(c, int) and c == 0):
                    act.wait_ge(prob_ready, c)
                for hl in range(2):
                    for s, (lo, hi) in enumerate(((0, P), (P, 3 * P))):
                        last = fn(EX[:, hl, lo:hi], SC[:, hl, lo:hi], ACT.Exp, bias=NMX[:, hl, s:s + 1],
                                  accum_out=SUM[:, hl, s:s + 1])
                last.then_inc(exp_ready, 1)
                if nxt is not None:
                    attend_in(*nxt)
                act.wait_ge(probT_psum, c + 1)
                if not (isinstance(c, int) and c == 0):
                    act.wait_ge(att_psum, c)
                for hl in range(2):
                    last = fn(PT[:, hl], PS[4 + hl][:, 0:3 * P], ACT.Copy)
                last.then_inc(probT_sbuf, 1)
                act.wait_ge(att_psum, c + 1)
                dst = B[1][:, c] if isinstance(c, int) else B[1][:, bass.ds(c, 1)].rearrange("p a t -> p (a t)")
                fn(dst, PS[6][:, 0:TT], ACT.Copy).then_inc(att_sbuf, 1)

            attend_in(0, 0)
            attend(0, (1, 1))
            with act.Fori(0, 3) as i:
                attend(2 * i + 1, (2 * i + 2, 0))
                attend(2 * i + 2, (2 * i + 3, 1))
            attend(7, None)
            wo_out(1)
            norm(7, XT)
            act.wait_ge(hn_psum, 1)
            for b in range(4):
                last = fn(HN[:, b // 2, 512 * (b % 2):512 * (b % 2) + 512], PS[b], ACT.Copy)
            last.then_inc(hn_sbuf, 1)
            act.wait_ge(logit_ready, 1)
            fn(RT["EXL"], RT["LG"], ACT.Exp).then_inc(logit_exp, 1)

            def gathered(j):
                act.wait_ge(gather_psum, j + 1)
                for b in range(2):
                    last = fn(XHI[:, 4 * b:4 * b + 4, 0:SLOTS], PS[1 + 2 * b].rearrange("p (c s) -> p c s", c=4),
                              ACT.Copy)
                last.then_inc(xhi_ready, 1)

            def job(j):
                hidden = swiglu("exp", NS * j + NS, j, 1)
                hidden(NS - 1)
                split("exp", 2 * FFN_LOADS, j)
                gathered(j + 1)
                split("exp", 2 * FFN_LOADS + 1, j)
                act.wait_ge(lo_used, 2 * FFN_LOADS * (j + 1) + UNITS["exp"])
                for half in range(2):
                    last = fn(YNAT[:, 0, 512 * half:512 * half + 512], PS[4 + half], ACT.Copy)
                last.then_inc(ey_sbuf, 1)

            gathered(0)
            for u in range(AHEAD):
                split("exp", u)
            with act.Fori(0, NE) as j:
                job(j)
            act.wait_ge(jobs_ready, 1)
            over = act.value_load(JOBI[0:1, NJ:NJ + 1], min_val=0, max_val=NOVER)
            with act.Fori(0, over) as j:
                job(j + NE)
            act.wait_ge(moe_done, 1)
            norm(8, ACC)

        @block.gpsimd
        def _(pool):
            order = Order(pool, pool_order)
            tt = nc.gpsimd.tensor_tensor

            def prep_keys(c, p):
                pool.wait_ge(prep_act, 4 * c + 1)
                if not (isinstance(c, int) and c == 0):
                    pool.wait_ge(prep_psum, 6 * (c - 1) + 5)
                pool.wait_ge(prep_dve, 6 * c + 1)
                kk = PP[p][:, 4:5].to_broadcast([P, TT])
                order(tt(KKR, RKV[:, 1], kk, ALU.mult))
                tt(SQ, KKR, KKR, ALU.mult).then_inc(prep_pool, 1)

            def prep_shift(c):
                pool.wait_ge(prep_dve, 6 * c + 3)
                tt(CUX, CUM, LD, ALU.subtract).then_inc(prep_pool, 1)

            def prep_factors(c, p):
                first = isinstance(c, int) and c < 2
                pool.wait_ge(prep_act, 4 * c + 4)
                if not first:
                    pool.wait_ge(gn_psum, 3 * (c - 2) + 1)
                if not (isinstance(c, int) and c == 0):
                    for e in range(2):
                        pool.wait_ge(chain_psum[e], CH * (c - 1) + 3)
                if not (isinstance(c, int) and c == 0):
                    pool.wait_ge(prep_psum, 6 * c)
                pool.wait_ge(prep_dve, 6 * c + 4)
                kin = THW
                for e in range(2):
                    order(tt(kin[:, e], kin[:, e], RKV[:, 1], ALU.mult))
                    order(tt(THA[:, e], THA[:, e], KKN, ALU.mult))
                    tt(AR[p][e][:, 0], KKN, PX[:, e], ALU.mult)
                    tt(AR[p][e][:, 1], RKV[:, 0], PW[:, e], ALU.mult)
                    tt(BT[p][:, e], THA[:, e], PINV[:, e], ALU.mult)
                    order(tt(KT[p][:, e], kin[:, e], PINV[:, e], ALU.mult))
                    end = T - 1 if e == 0 else 0
                    last = PW[:, e, end:end + 1].to_broadcast([P, T])
                    tt(HATT[:, 2 * e], BT[p][:, e, 0:T], last, ALU.mult)
                    order(tt(HATT[:, 2 * e + 1], KT[p][:, e, 0:T], last, ALU.mult))
                order(tt(COEF, kin[:, 0], kin[:, 1], ALU.add))
                order(tt(COEF, COEF, RKV[:, 0], ALU.mult))
                tt(COEF, COEF, PP[p][:, 7:8].to_broadcast([P, TT]), ALU.mult).then_inc(prep_pool, 1)

            def prep(c, p):
                prep_keys(c, p)
                prep_shift(c)
                prep_factors(c, p)

            prep(0, 0)
            prep(1, 1)
            with pool.Fori(0, 3) as i:
                order.enter(i, STEPS_POOL_MIX)
                prep(2 * i + 2, 0)
                prep(2 * i + 3, 1)
                order.leave(3)

            pool.wait_ge(h_ready, 3)
            for p in range(2):
                nc.gpsimd.memset(BIAS[p][:, :, 0:P], 0.0)
                order(nc.gpsimd.memset(BIAS[p][:, :, 2 * P:3 * P], 0.0))

            def bias(c, r, p):
                pool.wait_ge(actx_full[p], 16 * (r + 1))
                if not isinstance(c, int) or c >= 2:
                    pool.wait_ge(score_ready, 2 * (c - 1))
                raw = W[:, HALF * p + BLK:HALF * p + BLK + 2 * P].rearrange("p (h k) -> p h k", h=2)
                tt(BIAS[p][:, :, P:2 * P], raw, con("window").unsqueeze(1).to_broadcast([P, 2, P]), ALU.add)\
                    .then_inc(bias_ready, 1)

            def leave(c, p):
                pool.wait_ge(qkv_sbuf, 2 * c + 2)
                for name, src in (("out_k", QK[p][:, 1, 0:T]), ("out_v", VA[p][:, 0])):
                    dst = a[name][c] if isinstance(c, int) else a[name][bass.ds(c, 1)].rearrange("a p n -> (a p) n")
                    pool.dma_start(dst, src).then_inc(kv_out[p], 16)

            for c in range(2):
                bias(c, 0, c)
                leave(c, c)
            with pool.Fori(0, 3) as i:
                for p in range(2):
                    bias(2 * i + 2 + p, i + 1, p)
                    leave(2 * i + 2 + p, p)

        @block.vector
        def _(dve):
            order = Order(dve, dve_order)
            tt, ts, stt = nc.vector.tensor_tensor, nc.vector.tensor_scalar, nc.vector.scalar_tensor_tensor
            nc.vector.memset(BIASES[:, 0:1], RMS_EPS)
            nc.vector.memset(BIASES[:, 2:3], -0.5 * DECAY)
            nc.vector.memset(BIASES[:, 3:4], -0.5)
            nc.vector.memset(BIASES[:, 1:2], GN_EPS).then_inc(eps_ready, 1)

            def split(phase, u, j=0):
                at = 2 * FFN_LOADS * j + UNITS[phase] + u
                dve.wait_ge(hi_ready, at + 1)
                if not isinstance(at, int) or at >= NBUF:
                    dve.wait_ge(lo_used, at - NBUF + 1)
                tt(LO[:, u % NBUF], raw_unit(phase, u), HI[:, u % NBUF].bitcast(F32), ALU.subtract)\
                    .then_inc(lo_ready, 1)

            def condition(l):
                nc.vector.memset(XHI.bitcast(F32)[:, :, 0:P], 0.0).then_inc(cond_hi, 1)
                dve.wait_ge(cond_hi, 2 * l + 2)
                tt(XHI[:, :, G:2 * G], COND, XHI[:, :, 0:G].bitcast(F32), ALU.subtract).then_inc(cond_split, 1)


            def gains(l):
                dve.wait_ge(col_in, 16)
                dve.wait_ge(mod_psum, MOD_TILES * (l + 1))
                b = col(f"mod_b{l}").unsqueeze(2).to_broadcast([P, 6 * C, G])
                order(tt(MOD[:, l], PS[2][:, 0:12 * C].rearrange("p (j g) -> p j g", g=G), b, ALU.add))
                for n, (name, at, add) in enumerate((("pre_mix", 1, 1.0), ("post_mix", 2, 0.0), ("pre_ffn", 4, 1.0),
                                                     ("post_ffn", 5, 0.0))):
                    g = col(f"{name}{l}").unsqueeze(2).to_broadcast([P, C, G])
                    last = stt(GAIN[:, l, n], MOD[:, l, C * at:C * at + C], add, g, ALU.add, ALU.mult)
                last.then_inc(mod_ready, 1)
                dve.wait_ge(mod_ready, l + 1)

            def norm_pre(n, l, k):
                dve.wait_ge(root_ready, n)
                order(nc.vector.reciprocal(RSTD, RMS))
                order(tt(B[1], XT, RSTD.unsqueeze(1).to_broadcast([P, C, TT]), ALU.mult))
                for c in range(C):
                    for g in range(G):
                        cs = slice(T * g, T * g + T)
                        last = ts(HT[:, c, cs], B[1][:, c, cs], GAIN[:, l, k, c, g:g + 1],
                                  MOD[:, l, (0 if k == 0 else 3) * C + c, g:g + 1], ALU.mult, ALU.add)
                last.then_inc(h_ready, 1)

            def norm_post(n, l, k, src, order=order):
                dve.wait_ge(root_ready, n)
                order(nc.vector.reciprocal(RSTD, RMS))
                order(tt(B[1], src, RSTD.unsqueeze(1).to_broadcast([P, C, TT]), ALU.mult))
                for c in range(C):
                    for g in range(G):
                        cs = slice(T * g, T * g + T)
                        last = stt(XT[:, c, cs], B[1][:, c, cs], GAIN[:, l, k, c, g:g + 1], XT[:, c, cs],
                                   ALU.mult, ALU.add)
                    if c % 2:
                        last.then_inc(x_ready, 1)

            condition(0)
            for u in range(2 * MOD_LOADS):
                split("mod0", u)
            gains(0)
            for n, (name, at, f, b) in enumerate((("w0", 0, 0.5, 0.0), ("w0", C, 0.5, 0.0), ("a0", 0, 0.5, 0.0),
                                                  ("a0", C, 0.5, 0.0), ("k_k", 0, 1.0, 0.0), ("k_a", 0, 0.5, 0.0),
                                                  ("k_a", 0, -0.5, 1.0), ("r_k", 0, 1.0, 0.0),
                                                  ("lnx_w", 0, 1.0, 0.0), ("lnx_b", 0, 1.0, 0.0))):
                last = ts(PAIR[:, :, n], col(name)[:, at:at + C], f, b, ALU.mult, ALU.add)
            order(last)
            norm_pre(1, 0, 0)
            dve.wait_ge(h_ready, 1)
            hh = HT.rearrange("p c (g t) -> p (c g) t", g=G)
            xx = XX.rearrange("p (n t) -> p n t", t=T)
            tt(xx[:, :, 1:T - 1], hh[:, :, 0:T - 2], hh[:, :, 2:T], ALU.add)
            nc.vector.tensor_copy(xx[:, :, 0:1], hh[:, :, 1:2])
            order(nc.vector.tensor_copy(xx[:, :, T - 1:T], hh[:, :, T - 2:T - 1]))
            order(stt(xx, xx, 0.5, hh, ALU.mult, ALU.subtract))
            xc = XX.rearrange("p (c t) -> p c t", c=C)
            for n, v in enumerate((1, 4, 5, 0, 2, 3)):
                if n >= 3:
                    dve.wait_ge(hid_psum, n - 2)
                for c in range(C):
                    last = stt(B[n % 3][:, c], xc[:, c], col("mu")[:, C * v + c:C * v + c + 1], HT[:, c],
                               ALU.mult, ALU.add)
                last.then_inc(mixed_ready, 1)
            dve.wait_ge(mixed_ready, 6)

            def prep_params(c, r, p):
                dve.wait_ge(pair_full[p], 16 * (r + 1))
                if not isinstance(c, int) or c >= 2:
                    dve.wait_ge(z_ready, c - 1)
                cs = slice(c, c + 1) if isinstance(c, int) else bass.ds(c, 1)
                s0 = W[:, HALF * p + BLK + 384:HALF * (p + 1)].rearrange("p (e i) -> p e i", e=2)
                ts(S0P[p], s0, float(np.exp(-CENTRE)), None, ALU.mult)
                nc.vector.tensor_copy(PP[p].unsqueeze(1), PAIR[:, cs]).then_inc(prep_dve, 1)

            def prep_floor(c):
                dve.wait_ge(prep_psum, 6 * c + 4)
                ts(SQ, PS[6][:, 0:TT], 1e-24, None, ALU.max).then_inc(prep_dve, 1)

            def prep_unit(c):
                dve.wait_ge(prep_act, 4 * c + 3)
                order(nc.vector.reciprocal(RROOT, ROOT))
                stt(KKN, KKR, -1.0, RROOT, ALU.mult, ALU.mult).then_inc(prep_dve, 1)

            def prep_scan(c):
                dve.wait_ge(prep_act, 4 * c + 2)
                for e in range(2):
                    for g in range(G):
                        cs = slice(T * g, T * g + T)
                        x, y = LD[:, e, cs], CUM[:, e, cs]
                        if e:
                            x, y = x[:, ::-1], y[:, ::-1]
                        last = nc.vector.tensor_tensor_scan(y, ONES, x, CENTRE, ALU.mult, ALU.add)
                last.then_inc(prep_dve, 1)

            def prep_bonus(c, p):
                dve.wait_ge(prep_psum, 6 * c + 5)
                tt(BONUS[p], PS[6][:, 0:TT], RKV[:, 2], ALU.mult)
                nc.vector.tensor_copy(VN[p], PS[6][:, TT:2 * TT].rearrange("p (g i) -> p g i", g=G))\
                    .then_inc(prep_dve, 1)

            def prep_hat(c, p):
                dve.wait_ge(prep_psum, 6 * c + 6)
                nc.vector.tensor_copy(HATN[p], PS[6].rearrange("p (n j) -> p n j", n=4)).then_inc(prep_dve, 1)

            def gram(e, c, k):
                dve.wait_ge(chain_psum[e], CH * c + k)
                if k < 3:
                    dst = (GB if k == 1 else GK)[e]
                    m = SEEN[:, e].rearrange("p k t -> p (k t)").unsqueeze(1).to_broadcast([P, 2, 2 * P])
                    for hl in range(2):
                        last = tt(dst[:, 2 * hl:2 * hl + 2].rearrange("p q k t -> p q (k t)"),
                                  PS[2 * e + hl].rearrange("p (q x) -> p q x", q=2), m, ALU.mult)
                    last.then_inc(chain_sbuf[e], 1)
                    return
                for hl in range(2):
                    tt(TN[e][:, 2 * hl:2 * hl + 2], PS[2 * e + hl][:, 0:2 * P].rearrange("p (q t) -> p q t", q=2),
                       PAIRM[:, e].unsqueeze(1).to_broadcast([P, 2, P]), ALU.mult)
                order(tt(TR[e], GB[e][:, :, 0], PAIRT[:, e].unsqueeze(1).to_broadcast([P, 4, P]), ALU.mult))
                eye = IDENT.unsqueeze(1).to_broadcast([P, 4, P])
                tt(TN[e], TN[e], eye, ALU.add).then_inc(natural_sbuf[e], 1)
                tt(TR[e], TR[e], eye, ALU.add).then_inc(chain_sbuf[e], 1)

            def level_z(e, c, n):
                dve.wait_ge(chain_psum[e], CH * c + 2 * n + 2)
                tt(Z[e], PS[2 * e].rearrange("p (q t) -> p q t", q=4),
                   LEVEL[:, e, n - 1].unsqueeze(1).to_broadcast([P, 4, P]), ALU.mult).then_inc(chain_sbuf[e], 1)

            def level_d(e, c, n):
                if n < 5:
                    dve.wait_ge(natural_psum[e], 4 * c + n)
                    tt(TN[e], TN[e], PS[2 * e].rearrange("p (q t) -> p q t", q=4), ALU.add)\
                        .then_inc(natural_sbuf[e], 1)
                dve.wait_ge(chain_psum[e], CH * c + 2 * n + 3)
                tt(TR[e], TR[e], PS[2 * e + 1].rearrange("p (q t) -> p q t", q=4), ALU.add)\
                    .then_inc(chain_sbuf[e], 1)

            def solve2(e, c):
                then = slice(64, 128) if e == 0 else slice(0, 64)
                dve.wait_ge(chain_psum[e], CH * c + 17)
                tt(U[e][then], U[e][then], PS[2 * e][then, 0:4 * N].rearrange("p (q i) -> p q i", q=4), ALU.add)\
                    .then_inc(chain_sbuf[e], 1)

            def gn_centre(c):
                dve.wait_ge(gn_psum, 3 * c + 2)
                order(stt(YC, PS[7][:, 0:TT], -1.0 / N, YT, ALU.mult, ALU.add))
                tt(YQ, YC, YC, ALU.mult).then_inc(gn_sbuf, 1)

            def gn_tail(c, p):
                dve.wait_ge(gn_root, c + 1)
                order(nc.vector.reciprocal(YS, YR))
                order(tt(YS, YC, YS, ALU.mult))
                order(ts(YS, YS, PP[p][:, 8:9], PP[p][:, 9:10], ALU.mult, ALU.add))
                order(tt(YS, YS, BONUS[p], ALU.add))
                dst = HT[:, c] if isinstance(c, int) else HT[:, bass.ds(c, 1)].rearrange("p a t -> p (a t)")
                tt(dst, YS, GATE[p], ALU.mult).then_inc(z_ready, 1)

            def mix_step(c, p, prep, tail):
                for e in range(2):
                    gram(e, c, 1)
                if tail:
                    gn_centre(c - 1)
                if tail:
                    gn_tail(c - 1, 1 - p)
                if prep is not None:
                    prep_params(prep[0], prep[2], prep[1])
                for e in range(2):
                    gram(e, c, 2)
                for e in range(2):
                    gram(e, c, 3)
                if prep is not None:
                    prep_floor(prep[0])
                    prep_scan(prep[0])
                for n in range(1, 6):
                    for e in range(2):
                        level_z(e, c, n)
                    for e in range(2):
                        level_d(e, c, n)
                    if prep is not None and n == 1:
                        prep_unit(prep[0])
                    if prep is not None and n == 4:
                        prep_bonus(*prep[:2])
                if prep is not None:
                    prep_hat(*prep[:2])
                for e in range(2):
                    solve2(e, c)

            prep_params(0, 0, 0)
            prep_floor(0)
            prep_scan(0)
            prep_unit(0)
            prep_bonus(0, 0)
            prep_hat(0, 0)
            mix_step(0, 0, (1, 1, 0), False)
            with dve.Fori(0, 3) as i:
                order.enter(i, STEPS_DVE_MIX)
                mix_step(2 * i + 1, 1, (2 * i + 2, 0, i + 1), True)
                mix_step(2 * i + 2, 0, (2 * i + 3, 1, i + 1), True)
                order.leave(3)
            mix_step(7, 1, None, True)
            gn_centre(7)
            gn_tail(7, 1)
            norm_post(2, 0, 1, B[0])
            norm_pre(3, 0, 2)

            def swiglu(phase, base, j, groups):
                width = T * groups

                def gated(s):
                    dve.wait_ge(sg_ready, base + s + 1)
                    if not (phase == "ffn" and s == 0):
                        dve.wait_ge(ht_psum, base + s)
                    for g in range(groups):
                        last = tt(HM[:, g], SG[:, g], PS[2 * (s % 2) + g][:, FB:2 * FB], ALU.mult)
                    last.then_inc(hm_ready, 1)

                def hidden(s):
                    dve.wait_ge(hhi_ready, base + s + 1)
                    tt(HLO[:, :, 0:width], PS[2 * (s % 2)][:, 0:2 * width].rearrange("p (f t) -> p f t", f=2),
                       HHI[:, :, 0:width].bitcast(F32), ALU.subtract).then_inc(hlo_ready, 1)

                for s in range(NS):
                    for n in range(4):
                        if phase == "ffn" or gu_unit(s, n) >= AHEAD:
                            split(phase, gu_unit(s, n), j)
                        if n == 0 and s:
                            gated(s - 1)
                    if s:
                        hidden(s - 1)
                        for f in range(2):
                            split(phase, down_unit(s - 1, f), j)
                gated(NS - 1)
                for f in range(2):
                    split(phase, down_unit(NS - 1, f), j)
                return hidden

            dve.wait_ge(xhi_ready, 1)
            tt(XLO, HT, XHI.bitcast(F32), ALU.subtract).then_inc(x_split, 1)
            swiglu("ffn", 0, 0, G)(NS - 1)
            norm_post(4, 0, 3, B[0])
            condition(1)
            for u in range(2 * MOD_LOADS):
                split("mod1", u)
            gains(1)
            norm_pre(5, 1, 0)

            def attend(c, p):
                dve.wait_ge(score_psum, c + 1)
                dve.wait_ge(bias_ready, c + 1)
                if not (isinstance(c, int) and c == 0):
                    dve.wait_ge(exp_ready, c)
                for hl in range(2):
                    last = stt(SC[:, hl], PS[2 + hl][:, 0:3 * P], SCALE, BIAS[p][:, hl], ALU.mult, ALU.add)
                last.then_inc(score_ready, 1)
                dve.wait_ge(score_ready, 2 * c + 1)
                nc.vector.reduce_max(MX[:, :, 0:1], SC[:, :, 0:P], AX)
                order(nc.vector.reduce_max(MX[:, :, 1:2], SC[:, :, P:3 * P], AX))
                ts(NMX, MX, -1.0, None, ALU.mult).then_inc(score_ready, 1)
                dve.wait_ge(exp_ready, c + 1)
                order(nc.vector.reciprocal(RSUM, SUM))
                if not (isinstance(c, int) and c == 0):
                    dve.wait_ge(probT_psum, c)
                for hl in range(2):
                    for s, (lo, hi) in enumerate(((0, P), (P, 3 * P))):
                        last = ts(PN[:, hl, lo:hi], EX[:, hl, lo:hi], RSUM[:, hl, s:s + 1], None, ALU.mult)
                last.then_inc(prob_ready, 1)

            attend(0, 0)
            with dve.Fori(0, 3) as i:
                order.enter(i, STEPS_DVE_ATT)
                attend(2 * i + 1, 1)
                attend(2 * i + 2, 0)
                order.leave(3)
            attend(7, 1)
            norm_post(6, 1, 1, B[0])
            norm_pre(7, 1, 2)

            lg, ex, pr, ra, oh1, pr2, oh2, chs, wt, pm = (RT[n] for n in names)

            def wide(x):
                return x.unsqueeze(2).to_broadcast([P, G, NE])

            def both(x):
                return x.unsqueeze(1).to_broadcast([P, G, NE])

            dve.wait_ge(logit_psum, 1)
            order(tt(lg, PS[4][:, 0:G * NE].rearrange("p (g e) -> p g e", g=G), both(col("router_b")), ALU.add))
            order(nc.vector.reduce_max(R2[0], lg, AX))
            tt(lg, lg, wide(R2[0]), ALU.subtract).then_inc(logit_ready, 1)
            dve.wait_ge(logit_exp, 1)
            order(nc.vector.reduce_sum(R2[1], ex, AX))
            order(nc.vector.reciprocal(R2[2], R2[1]))
            order(tt(pr, ex, wide(R2[2]), ALU.mult))

            def first_largest(out, x, m, v):
                order(nc.vector.reduce_max(m, x, AX))
                order(tt(ra, x, wide(m), ALU.is_equal))
                order(tt(ra, ra, both(con("expert_rank")), ALU.mult))
                order(nc.vector.reduce_max(v, ra, AX))
                order(tt(out, ra, wide(v), ALU.is_equal))

            first_largest(oh1, pr, R2[3], R2[4])
            order(stt(pr2, oh1, -2.0, pr, ALU.mult, ALU.add))
            first_largest(oh2, pr2, R2[3], R2[4])
            order(tt(chs, oh1, oh2, ALU.add))
            tt(wt, pr, chs, ALU.mult).then_inc(chosen, 1)
            dve.wait_ge(chosen, 1)
            order(nc.vector.reduce_sum(R2[5], wt, AX))
            order(nc.vector.reciprocal(R2[6], R2[5]))
            nc.vector.memset(JOBP, -1.0)
            nc.vector.memset(JOBW, 0.0)
            order(nc.vector.memset(JOBE, 0.0))
            order(tt(JOBW[:, :, 0:NE], wt, wide(R2[6]), ALU.mult))
            dve.wait_ge(place_psum, 1)
            order(tt(pm, PS[5][:, 0:G * NE].rearrange("p (g e) -> p g e", g=G), chs, ALU.mult))
            order(ts(ra, chs, -1.0, 1e6, ALU.add, ALU.mult))
            order(tt(pm, pm, ra, ALU.add))
            nc.vector.tensor_copy(JOBP[:, :, 0:NE], pm)
            order(ts(CNT[:, 0], PS[5][:, 2 * NE:3 * NE], SLOTS + 0.5, None, ALU.is_gt))
            order(nc.vector.tensor_tensor_scan(CNT[:, 1], ONES[:, 0:NE], CNT[:, 0], 0.0, ALU.mult, ALU.add))
            order(tt(CNT[:, 2], CNT[:, 1], CNT[:, 0], ALU.subtract))
            order(ts(pm, pm, -float(SLOTS), None, ALU.add))
            for k in range(NOVER):
                order(stt(CNT[:, 3], CNT[:, 2], float(k), CNT[:, 0], ALU.is_equal, ALU.mult))
                order(tt(JT, both(CNT[:, 3]), pm, ALU.mult))
                order(nc.vector.reduce_sum(JOBP[:, :, NE + k:NE + k + 1], JT, AX))
                order(tt(JT, both(CNT[:, 3]), JOBW[:, :, 0:NE], ALU.mult))
                order(nc.vector.reduce_sum(JOBW[:, :, NE + k:NE + k + 1], JT, AX))
                order(tt(CNT[:, 3], CNT[:, 3], con("expert"), ALU.mult))
                order(nc.vector.reduce_sum(JOBE[:, NE + k:NE + k + 1], CNT[:, 3], AX))
            nc.vector.tensor_copy(JOBI[:, 0:NJ], JOBE)
            nc.vector.tensor_copy(JOBI[:, NJ:NJ + 1], CNT[:, 1, NE - 1:NE]).then_inc(jobs_ready, 1)

            def select(j):
                js = slice(j, j + 1) if isinstance(j, int) else bass.ds(j, 1)
                for g in range(G):
                    last = ts(SEL[:, g], con("slot"), JOBP[:, g, js], None, ALU.is_equal)
                order(last)
                for g in range(G):
                    last = ts(SELW[:, g], SEL[:, g], JOBW[:, g, js], None, ALU.mult)
                last.then_inc(sel_ready, 1)

            def weights_turned(j):
                dve.wait_ge(selT_psum, j + 1)
                nc.vector.tensor_copy(SELWT, PS[2][:, 0:TT]).then_inc(selT_sbuf, 1)

            def gathered(j):
                dve.wait_ge(xhi_ready, j + 2)
                for b in range(2):
                    last = tt(XLO[:, 4 * b:4 * b + 4, 0:SLOTS], PS[1 + 2 * b].rearrange("p (c s) -> p c s", c=4),
                              XHI[:, 4 * b:4 * b + 4, 0:SLOTS].bitcast(F32), ALU.subtract)
                last.then_inc(x_split, 1)

            def job(j):
                select(j + 1)
                hidden = swiglu("exp", NS * j + NS, j, 1)
                hidden(NS - 1)
                split("exp", 2 * FFN_LOADS, j)
                gathered(j + 1)
                split("exp", 2 * FFN_LOADS + 1, j)
                for b in range(4):
                    dve.wait_ge(scat_psum, 4 * j + b + 1)
                    part = ACC[:, 2 * b:2 * b + 2]
                    tt(part, part, PS[(6, 7, 1, 3)[b]].rearrange("p (c t) -> p c t", c=2), ALU.add)\
                        .then_inc(scat_acc, 1)
                weights_turned(j + 1)

            nc.vector.memset(ACC, 0.0).then_inc(scat_acc, 1)
            dve.wait_ge(scat_acc, 1)
            select(0)
            gathered(0)
            for u in range(AHEAD):
                split("exp", u)
            weights_turned(0)
            with dve.Fori(0, NE) as j:
                order.enter(j, STEPS_DVE_JOB)
                job(j)
                order.leave(NE)
            over = dve.value_load(JOBI[0:1, NJ:NJ + 1], min_val=0, max_val=NOVER)
            with dve.Fori(0, over) as j:
                order.enter(j, STEPS_DVE_JOB)
                job(j + NE)
            nc.vector.memset(RT["LG"], 0.0).then_inc(moe_done, 1)
            norm_post(8, 1, 3, ACC, Order(dve, last_order))


def pack(x):
    f = {n: np.asarray(v) for n, v in x.items()}

    def cols(v):
        v = v.reshape(-1, C, P)
        return v.transpose(2, 0, 1).reshape(P, -1)

    def tiles(w):
        k, m = w.shape
        return w.reshape(k // P, P, m // P, P).transpose(1, 2, 0, 3)

    c = {}
    for l in range(2):
        for n in ("mix_pre", "mix_post", "ffn_pre", "ffn_post"):
            kind, when = n.split("_")
            c[f"{when}_{kind}{l}"] = cols(f[f"l{l}_norm_{n}"])
        c[f"mod_b{l}"] = cols(f[f"l{l}_mod_b"])
    for n in ("mu", "w0", "a0", "k_k", "k_a", "lnx_w", "lnx_b"):
        c[n] = cols(f["l0_" + n])
    c["r_k"] = cols(f["l0_r_k"].reshape(D))
    c["cond"] = np.stack([f["c_ctx"], f["c"][0]], 1).reshape(C, P, G).transpose(1, 0, 2).reshape(P, -1)
    c["router_w"] = f["l1_router_w"].reshape(C, P, NE).transpose(1, 0, 2).reshape(P, -1)
    c["router_b"] = np.broadcast_to(f["l1_router_b"], (P, NE))
    out = {"cols": np.concatenate([c[n] for n in COLS], 1)}
    out["cons"] = shape_constants()
    tok = np.concatenate([f["x_prompt"][0], f["x_sample"][0]], 0)
    out["x"] = tok.reshape(TT, C, P).transpose(2, 1, 0)

    def moving(w, width):
        k, m = w.shape
        return w.reshape(k // P, P, m // width, width).transpose(2, 1, 0, 3).reshape(m // width, P, -1)

    def in_loads(w):
        return w.reshape(len(w), P, -1, LOAD).transpose(0, 2, 1, 3).reshape(-1, P, LOAD)

    s0 = f["state_l0"][0].reshape(2, C, 2, N, N)
    s0 = s0.transpose(1, 2, 4, 0, 3).reshape(C, P, 2 * N)
    out["w_mod"] = np.stack([in_loads(moving(f[f"l{l}_mod_w"], 512)) for l in range(2)])
    e1 = [f[n].transpose(1, 0, 2).reshape(D, P) for n in ("l0_w1", "l0_a1")] + [f["l0_g1"]]
    out["w_lora"] = np.concatenate([tiles(w).reshape(P, D) for w in e1], 1)
    rkv = [tiles(f["l0_" + n]) for n in ("wr", "wk", "wv")]
    e2 = [f[n].reshape(P, C, P) for n in ("l0_w2", "l0_a2", "l0_g2")]
    out["w_rkv"] = np.stack([np.concatenate([w[:, j].reshape(P, D) for w in rkv] + [w[:, j] for w in e2] + [s0[j]], 1)
                             for j in range(C)])
    out["w_o"] = np.stack([tiles(f[f"l{l}_wo"]).reshape(P, C * D) for l in range(2)])

    def swiglu(wg, wu, wd):
        gu = in_loads(np.concatenate([moving(w, FB).reshape(NS, P, C, FB) for w in (wg, wu)], 3).reshape(NS, P, -1))
        dn = wd.reshape(NS, 2, P, D).transpose(0, 2, 1, 3).reshape(NS, P, LOAD)
        steps = [gu[0:2]] + [x for s in range(1, NS) for x in (gu[2 * s:2 * s + 2], dn[s - 1:s])] + [dn[NS - 1:]]
        return np.concatenate(steps, 0)

    out["w_ffn"] = swiglu(f["l0_ffn_wg"], f["l0_ffn_wu"], f["l0_ffn_wd"])
    out["w_exp"] = np.stack([swiglu(f["l1_exp_wg"][e], f["l1_exp_wu"][e], f["l1_exp_wd"][e]) for e in range(NE)])
    tq, tk = np.arange(T)[:, None], np.arange(T)[None]
    ridx = tk // GRID_W - tq // GRID_W + 7
    cidx = np.clip(tk % GRID_W - tq % GRID_W + WIN_W - 1, 0, 2 * WIN_W - 2)
    rel = f["l1_rpb"][:, ridx, cidx].reshape(C, 2, T, T).transpose(0, 2, 1, 3).reshape(C, T, 2 * T)
    ck = f["cache_k_l1"][0].reshape(C, 2, T, N).transpose(0, 1, 3, 2).reshape(C, P, T)
    cv = f["cache_v_l1"][0].reshape(C, 2, T, N).transpose(0, 2, 1, 3).reshape(C, T, P)
    w = tiles(f["l1_wqkv"])
    out["w_qkv"] = np.stack([np.concatenate([w[:, C * n + j].reshape(P, D) for n in range(3)]
                                            + [rel[j], ck[j], cv[j]], 1) for j in range(C)])
    return {n: np.ascontiguousarray(v) for n, v in out.items()}


_OUTS = {"out_x": (P, C, TT), "out_state": (C, P, 2 * N), "out_k": (C, P, T), "out_v": (C, T, P)}


def unpack(r):
    x = r["out_x"].transpose(2, 1, 0).reshape(TT, D)
    s = r["out_state"].reshape(C, 2, N, 2, N).transpose(3, 0, 1, 2, 4).reshape(1, 2, H, N, N)
    k = r["out_k"].reshape(C, 2, N, T).transpose(0, 1, 3, 2).reshape(1, H, T, N)
    v = r["out_v"].reshape(C, T, 2, N).transpose(0, 2, 1, 3).reshape(1, H, T, N)
    return tuple(np.ascontiguousarray(o) for o in (x[None, 0:T], x[None, T:], s, k, v))


def kernel(**inputs):
    import concourse.bacc as _bacc
    from concourse import mybir as _mybir
    from concourse.bass_utils import run_bass_kernel_spmd as _run

    nc = _bacc.Bacc("TRN2", target_bir_lowering=False, num_devices=1)
    arrays = pack(inputs)
    aps = {n: nc.dram_tensor(n, v.shape, _mybir.dt.from_np(v.dtype), kind="ExternalInput").ap()
           for n, v in arrays.items()}
    for n, shape in _OUTS.items():
        aps[n] = nc.dram_tensor(n, shape, _mybir.dt.float32, kind="ExternalOutput").ap()
    build(nc, aps)
    r = _run(nc, [arrays], core_ids=[0])
    return unpack(r.results[0])
```
